# Optimizing a Trainium2 kernel written in Bass

```python
import jax, jax.numpy as jnp
from jax import lax
import numpy as np

D_MODEL = 2048
BATCH = 1
SEQ = 256
DEPTH = 2

CHUNK = 64
N_EVEN = (DEPTH + 1) // 2
N_ODD = DEPTH // 2

A_HEADS = 8
A_DK = 128
A_DV = 128
A_CONV = 4
B_GROUPS = 8
B_DG = 128
B_BLOCK = 128
A_QK = A_HEADS * A_DK
A_V = A_HEADS * A_DV
B_W = B_GROUPS * B_DG
A_QKV = 2 * A_QK + A_V
IN_COLS = A_QKV + A_V + 2 * A_HEADS + 2 * B_W
MIX_W = A_V + B_W
C_WIDTH = 31
D_FF = 4 * D_MODEL
EPS = 1e-6

kernel_name = "hybrid_deltanet_gmlp_conformer_block"

def rmsnorm(x, g):
    xf = x.astype(jnp.float32)
    y = xf * lax.rsqrt(jnp.mean(xf * xf, axis=-1, keepdims=True) + EPS)
    return (y * g.astype(jnp.float32)).astype(x.dtype)

def layernorm(x, g, b):
    xf = x.astype(jnp.float32)
    mu = jnp.mean(xf, axis=-1, keepdims=True)
    xc = xf - mu
    y = xc * lax.rsqrt(jnp.mean(xc * xc, axis=-1, keepdims=True) + EPS)
    return (y * g.astype(jnp.float32) + b.astype(jnp.float32)).astype(x.dtype)

def l2norm(x):
    return x * lax.rsqrt(jnp.sum(x * x, axis=-1, keepdims=True) + EPS)

def causal_dwconv(x, w):
    k = w.shape[0]
    return lax.conv_general_dilated(
        x, w[:, None, :].astype(x.dtype), window_strides=(1,), padding=[(k - 1, 0)],
        dimension_numbers=("NWC", "WIO", "NWC"), feature_group_count=x.shape[-1])

def gated_delta_rule(q, k, v, g, beta):
    bsz, seq, heads, dk = q.shape
    dv = v.shape[-1]
    n = seq // CHUNK

    def chunks(t):
        return jnp.moveaxis(t.astype(jnp.float32).reshape(bsz, n, CHUNK, heads, -1), 3, 1)

    q = chunks(q) * (dk ** -0.5)
    k = chunks(k)
    v = chunks(v)
    g = jnp.moveaxis(g.astype(jnp.float32).reshape(bsz, n, CHUNK, heads), 3, 1)
    beta = jnp.moveaxis(beta.astype(jnp.float32).reshape(bsz, n, CHUNK, heads), 3, 1)
    g = jnp.cumsum(g, axis=-1)

    tri = jnp.tril(jnp.ones((CHUNK, CHUNK), dtype=bool))
    strict = jnp.tril(jnp.ones((CHUNK, CHUNK), dtype=bool), -1)
    eye = jnp.eye(CHUNK, dtype=jnp.float32)
    decay = jnp.exp(jnp.where(tri, g[..., :, None] - g[..., None, :], -jnp.inf))

    k_beta = k * beta[..., None]
    v_beta = v * beta[..., None]
    a = jnp.einsum("bhnid,bhnjd->bhnij", k_beta, k) * decay
    a = jnp.where(strict, a, 0.0) + eye
    rhs = jnp.concatenate([v_beta, k_beta * jnp.exp(g)[..., None]], axis=-1)
    sol = lax.linalg.triangular_solve(a, rhs, left_side=True, lower=True, unit_diagonal=True)
    u = sol[..., :dv]
    w = sol[..., dv:]

    attn = jnp.einsum("bhnid,bhnjd->bhnij", q, k) * decay
    q_dec = q * jnp.exp(g)[..., None]
    k_tail = k * jnp.exp(g[..., -1:] - g)[..., None]
    g_last = jnp.exp(g[..., -1])

    xs = tuple(jnp.moveaxis(t, 2, 0) for t in (attn, q_dec, k_tail, u, w, g_last))

    def step(state, inp):
        attn_c, qd_c, kt_c, u_c, w_c, gl_c = inp
        v_new = u_c - jnp.einsum("bhck,bhkv->bhcv", w_c, state)
        o_c = (jnp.einsum("bhck,bhkv->bhcv", qd_c, state)
               + jnp.einsum("bhij,bhjv->bhiv", attn_c, v_new))
        state = state * gl_c[..., None, None] + jnp.einsum("bhck,bhcv->bhkv", kt_c, v_new)
        return state, o_c

    s0 = jnp.zeros((bsz, heads, dk, dv), jnp.float32)
    _, o = lax.scan(step, s0, xs)
    return jnp.transpose(o, (1, 0, 3, 2, 4)).reshape(bsz, seq, heads, dv)

def even_mixer(h, w_in, conv_w, a_log, dt_bias, o_norm, ln_g, ln_b, w_s, b_s, w_out):
    bsz, seq, _ = h.shape
    proj = h @ w_in.astype(h.dtype)
    cuts = [int(c) for c in np.cumsum([A_QKV, A_V, A_HEADS, A_HEADS, B_W])]
    qkv, z, b_raw, a_raw, u_raw, v_raw = jnp.split(proj, cuts, axis=-1)

    qkv = jax.nn.silu(causal_dwconv(qkv, conv_w))
    q, k, v = jnp.split(qkv, [A_QK, 2 * A_QK], axis=-1)
    q = l2norm(q.astype(jnp.float32).reshape(bsz, seq, A_HEADS, A_DK))
    k = l2norm(k.astype(jnp.float32).reshape(bsz, seq, A_HEADS, A_DK))
    v = v.reshape(bsz, seq, A_HEADS, A_DV)
    beta = jax.nn.sigmoid(b_raw.astype(jnp.float32))
    g = -jnp.exp(a_log.astype(jnp.float32)) * jax.nn.softplus(
        a_raw.astype(jnp.float32) + dt_bias.astype(jnp.float32))
    o = gated_delta_rule(q, k, v, g, beta)
    o = rmsnorm(o, o_norm) * jax.nn.silu(z.astype(jnp.float32).reshape(bsz, seq, A_HEADS, A_DV))
    out_a = o.reshape(bsz, seq, A_V).astype(h.dtype)

    u = jax.nn.gelu(u_raw, approximate=False)
    vg = jax.nn.gelu(v_raw, approximate=False).reshape(bsz, seq, B_GROUPS, B_DG)
    vg = layernorm(vg, ln_g.reshape(B_GROUPS, B_DG), ln_b.reshape(B_GROUPS, B_DG))
    vg = vg.reshape(bsz, seq // B_BLOCK, B_BLOCK, B_GROUPS, B_DG)
    pos = np.arange(B_BLOCK)
    mask = (pos[None, :] // CHUNK) <= (pos[:, None] // CHUNK)
    w_masked = jnp.where(mask, w_s, 0.0).astype(h.dtype)
    mixed = jnp.einsum("gij,bmjgc->bmigc", w_masked, vg) + b_s.T.astype(h.dtype)[None, None, :, :, None]
    out_b = u * mixed.reshape(bsz, seq, B_W)

    return jnp.concatenate([out_a, out_b], axis=-1) @ w_out.astype(h.dtype)

def conformer_conv(h, pw1, pw1_b, dw, dw_b, ln_g, ln_b, pw2, pw2_b):
    z = h @ pw1.astype(h.dtype) + pw1_b.astype(h.dtype)
    z = z[..., :D_MODEL] * jax.nn.sigmoid(z[..., D_MODEL:])
    z = causal_dwconv(z, dw) + dw_b.astype(h.dtype)
    z = jax.nn.silu(layernorm(z, ln_g, ln_b))
    return z @ pw2.astype(h.dtype) + pw2_b.astype(h.dtype)

def sq_relu_mlp(h, w1, w2):
    a = jax.nn.relu(h @ w1.astype(h.dtype))
    return (a * a) @ w2.astype(h.dtype)

def setup_inputs(seed: int = 0) -> dict:
    key = jax.random.key(seed)
    ks = iter(jax.random.split(key, 40))

    def nrm(shape, scale):
        return jax.random.normal(next(ks), shape, jnp.float32) * scale

    def gain(shape):
        return 1.0 + nrm(shape, 0.05)

    dt = jnp.exp(jax.random.uniform(next(ks), (N_EVEN, A_HEADS), jnp.float32,
                                    np.log(1e-3), np.log(1e-1)))
    return {
        "x": nrm((BATCH, SEQ, D_MODEL), 1.0),
        "e_norm": gain((N_EVEN, D_MODEL)),
        "e_w_in": nrm((N_EVEN, D_MODEL, IN_COLS), D_MODEL ** -0.5),
        "e_conv_w": nrm((N_EVEN, A_CONV, A_QKV), A_CONV ** -0.5),
        "e_a_log": jnp.log(jax.random.uniform(next(ks), (N_EVEN, A_HEADS), jnp.float32, 1.0, 16.0)),
        "e_dt_bias": dt + jnp.log(-jnp.expm1(-dt)),
        "e_o_norm": gain((N_EVEN, A_DV)),
        "e_ln_g": gain((N_EVEN, B_W)),
        "e_ln_b": nrm((N_EVEN, B_W), 0.02),
        "e_w_s": nrm((N_EVEN, B_GROUPS, B_BLOCK, B_BLOCK), B_BLOCK ** -0.5),
        "e_b_s": gain((N_EVEN, B_GROUPS, B_BLOCK)),
        "e_w_out": nrm((N_EVEN, MIX_W, D_MODEL), MIX_W ** -0.5),
        "o_norm": gain((N_ODD, D_MODEL)),
        "o_pw1": nrm((N_ODD, D_MODEL, 2 * D_MODEL), D_MODEL ** -0.5),
        "o_pw1_b": nrm((N_ODD, 2 * D_MODEL), 0.02),
        "o_dw": nrm((N_ODD, C_WIDTH, D_MODEL), C_WIDTH ** -0.5),
        "o_dw_b": nrm((N_ODD, D_MODEL), 0.02),
        "o_ln_g": gain((N_ODD, D_MODEL)),
        "o_ln_b": nrm((N_ODD, D_MODEL), 0.02),
        "o_pw2": nrm((N_ODD, D_MODEL, D_MODEL), D_MODEL ** -0.5),
        "o_pw2_b": nrm((N_ODD, D_MODEL), 0.02),
        "f_norm": gain((DEPTH, D_MODEL)),
        "f_w1": nrm((DEPTH, D_MODEL, D_FF), D_MODEL ** -0.5),
        "f_w2": nrm((DEPTH, D_FF, D_MODEL), D_FF ** -0.5),
        "final_norm": gain((D_MODEL,)),
    }

def reference(x, e_norm, e_w_in, e_conv_w, e_a_log, e_dt_bias, e_o_norm, e_ln_g, e_ln_b,
              e_w_s, e_b_s, e_w_out, o_norm, o_pw1, o_pw1_b, o_dw, o_dw_b, o_ln_g, o_ln_b,
              o_pw2, o_pw2_b, f_norm, f_w1, f_w2, final_norm):
    for layer in range(DEPTH):
        i = layer // 2
        if layer % 2 == 0:
            x = x + even_mixer(rmsnorm(x, e_norm[i]), e_w_in[i], e_conv_w[i], e_a_log[i],
                               e_dt_bias[i], e_o_norm[i], e_ln_g[i], e_ln_b[i], e_w_s[i],
                               e_b_s[i], e_w_out[i])
        else:
            x = x + conformer_conv(rmsnorm(x, o_norm[i]), o_pw1[i], o_pw1_b[i], o_dw[i],
                                   o_dw_b[i], o_ln_g[i], o_ln_b[i], o_pw2[i], o_pw2_b[i])
        x = x + sq_relu_mlp(rmsnorm(x, f_norm[layer]), f_w1[layer], f_w2[layer])
    return rmsnorm(x, final_norm)


_drawn_inputs = setup_inputs


def setup_inputs(seed=0):
    import zlib

    import numpy as np

    out = dict(_drawn_inputs(seed))
    spreads = {}
    factors = {'e_ln_g': 3.197,
     'e_ln_b': 8.0,
     'e_b_s': 2.762,
     'o_norm': 3.056,
     'o_pw1_b': 6.868,
     'o_dw_b': 4.007,
     'o_ln_g': 2.755,
     'o_ln_b': 8.0,
     'o_pw2_b': 5.099,
     'e_o_norm': 4.338}
    for name, (base, spread) in spreads.items():
        noise = np.random.default_rng([zlib.crc32(name.encode()), seed]).standard_normal(out[name].shape)
        drawn = base * np.exp(spread * noise) if base else spread * noise
        out[name] = __import__('jax').numpy.asarray(drawn.astype(out[name].dtype))
    for name, factor in factors.items():
        out[name] = (out[name] * factor).astype(out[name].dtype)
    return out
```

```python
from contextlib import ExitStack

import concourse.bass as bass
from concourse import mybir
from concourse.alu_op_type import AluOpType as ALU

F32 = mybir.dt.float32
F32R = mybir.dt.float32r
ACT = mybir.ActivationFunctionType
AX = mybir.AxisListType.X

P = 128
D = 2048
T = 256
KT = D // P
TT = T // P
H = 8
HH = 4
C = 64
NQ = 4
NB = 16
WD = 31
CH_K = 4
CH_N = 512
CH = CH_K * CH_N
RAW = 2
SPLIT = 2
G_QKVZ, G_UV, G_WOUT, G_MLP0, G_PW1, G_PW2, G_MLP1, G_END = 0, 8, 12, 16, 48, 56, 60, 92
EPS = 1e-6
QKVZ_AT = [0, 8, 16, 4, 12, 20, 24, 28]
LEVELS = 5

CONSTS = ["ident", "ones", "upto", "chunk", "fill", "strict", "lev0t"] + [f"lev{i}" for i in range(1, LEVELS + 1)]
PARAMS, _at = {}, 0
for _n, _w in (("e_norm", KT), ("f_norm0", KT), ("o_norm", KT), ("f_norm1", KT), ("final_norm", KT),
               ("pw1_b", 2 * KT), ("dw_b", KT), ("ln_g", KT), ("ln_b", KT), ("pw2_b", KT),
               ("head_norm", 1), ("a_log", H), ("dt_bias", H), ("eps", 1), ("eps_q", 1)):
    PARAMS[_n] = (_at, _at + _w)
    _at += _w
N_PARAMS = _at


def build(nc, xt, wts, w_ba, consts, params, conv_w, dw, rows, w_s, out):
    with ExitStack() as ctx:
        def sb(name, shape, dt=F32):
            return ctx.enter_context(nc.sbuf_tensor(name, shape, dt))

        def sem(name):
            return ctx.enter_context(nc.semaphore(name))

        used = (nc.sbuf_base + 63) // 64 * 64
        sb("arena", [P, 8192 + 4096 + 32])
        xg = nc.alloc_sbuf_tensor_at("xg", [P, KT, 2, T], F32R, offset=used)
        xg_space = nc.alloc_sbuf_tensor_at("xg_space", [P, 16, 512], F32, offset=used)
        x = nc.alloc_sbuf_tensor_at("x", [P, KT, T], F32, offset=used + 32768)
        x_space = nc.alloc_sbuf_tensor_at("x_space", [P, 8, 512], F32, offset=used + 32768)
        hid = sb("hid", [P, KT, 2, T], F32R)
        raw = sb("raw", [P, RAW, CH])
        whi = sb("whi", [P, SPLIT, CH_K, CH_N], F32R)
        wlo = sb("wlo", [P, SPLIT, CH_K, CH_N], F32R)
        work = sb("work", [P, 12288])
        cross = sb("cross", [P, CH_K, T])
        total = sb("total", [P, CH_K, T])
        padded = sb("padded", [P, CH_K, T + 4])
        ct = sb("ct", [P, len(CONSTS), P])
        pt = sb("pt", [P, N_PARAMS])
        cw = sb("cw", [P, 24, 4])
        dwt = sb("dwt", [P, KT, WD])
        rms = sb("rms", [P, T])
        ssum = sb("ssum", [P, T])
        sq_part = sb("sq_part", [P, T])
        wba_raw = sb("wba_raw", [P, KT, NB])
        wba = sb("wba", [P, KT, 2, NB], F32R)
        gates = sb("gates", [P, 8, TT, H])
        small = sb("small", [P, 16, TT, H])
        ps = ctx.enter_context(nc.psum_tensor("ps", [P, 8, 512], F32))

        def const(name):
            return ct[:, CONSTS.index(name), :]

        def param(name):
            a, b = PARAMS[name]
            return pt[:, a:b]

        acts = work[:].rearrange("p (n t) -> p n t", t=T)
        zpad = work[:, 0:KT * (T + 32)].rearrange("p (n t) -> p n t", t=T + 32)
        conv = work[:, 4608:4608 + KT * T].rearrange("p (n t) -> p n t", t=T)

        def bank(b):
            return ps[:, b, :].rearrange("p (h c) -> p h c", h=HH)

        def per_head(ap):
            return ap.unsqueeze(2).to_broadcast([P, HH, P])

        def all_heads(ap):
            return ap.unsqueeze(1).to_broadcast([P, HH, P])

        raw_in = [sem(f"raw_in{i}") for i in range(RAW)]
        const_in, x_in, rows_in, x_again = sem("const_in"), sem("x_in"), sem("rows_in"), sem("x_again")
        hi_ready, lo_ready = sem("hi_ready"), sem("lo_ready")
        chunk_free = sem("chunk_free")
        cross_ready = sem("cross_ready")
        banks_free = sem("banks_free")
        hid_scaled = sem("hid_scaled")
        xg_raw, xg_hi, xg_ready = sem("xg_raw"), sem("xg_hi"), sem("xg_ready")
        hid_raw, hid_hi, hid_ready = sem("hid_raw"), sem("hid_hi"), sem("hid_ready")
        x_part = sem("x_part")
        x_new = sem("x_new")
        sq_ready, ssum_part, ssum_ready = sem("sq_ready"), sem("ssum_part"), sem("ssum_ready")
        ms_ready, root_ready, rms_ready = sem("ms_ready"), sem("root_ready"), sem("rms_ready")
        scaled, out_raw, out_done = sem("scaled"), sem("out_raw"), sem("out_done")
        dve_step, act_step = sem("dve_step"), sem("act_step")
        names = ["wba_hi", "wba_ready", "ba_prod", "ba_cross", "ba_sum", "beta", "softplus", "g", "gc_prod", "gates",
                 "qkvz_raw", "qkvz_ready", "uv_ready",
                 "lg", "elast", "tok", "tok_sq", "ss", "root", "normed", "gb", "decay_in", "decay", "feat", "feat_dve", "feat_act",
                 "prods", "inv0", "t_prod", "t_copy", "y_prod", "z", "ut_prod", "u_copy", "w_prod", "w_copy", "state",
                 "v_prod", "v_copy", "s_prod", "o_sq", "o_ss", "o_root", "o_norm", "o_prod", "gated", "mix_hi", "mix_a",
                 "gv_prod", "gv_center", "gv_sq", "gv_ss", "gv_root", "gv_norm", "mixed", "gm_out", "gm_hi", "mix_b",
                 "glu_scaled", "gate", "glu", "tap", "ln_sum", "ln_mean", "ln_mu", "ln_center", "ln_sq", "ln_ss", "ln_ms",
                 "ln_root", "ln_rs", "ln_norm", "ln_act"]
        s = {n: sem(n) for n in names}
        block = ctx.enter_context(nc.Block())

        slots = [x_space[:, i, :] for i in range(8)] + [xg_space[:, i, :] for i in range(16)]
        buf = {n: slots[i].rearrange("p (h c) -> p h c", h=HH) for i, n in enumerate(
            ["lg", "kn", "qn", "vb", "kb", "kd", "kt", "qd", "knT", "kbT", "qnT", "qdT", "decay", "decay_s", "attnT",
             "C", "U", "T", "Z", "v_new", "state", "state_d"])}
        buf |= {"sq_k": buf["Z"], "sq_q": buf["T"], "o_n": buf["kn"], "gate_out": buf["qn"], "wT": buf["knT"],
                "o_sq": buf["kb"]}
        wide = {n: xg_space[:, 2 * i:2 * i + 2, :].rearrange("p b (g c) -> p (b g) c", g=HH) for i, n in enumerate(
            ["ln_g", "ln_b", "b_s", "w_s", "center", "sq", "mixed"])}
        elast = small[:, 0:4].rearrange("p a m h -> p (a m h)")[:, 0:8].rearrange("p (h c) -> p h c", c=2)
        flat_small = small[:].rearrange("p a m h -> p (a m h)")

        def sm(i, n=8):
            return flat_small[:, 16 + 8 * i:16 + 8 * i + n]

        def pair(b):
            return ps[:, b:b + 2, :].rearrange("p b (g c) -> p (b g) c", g=HH)

        def tok(m):
            return slice(P * m, P * m + P)

        @block.sync
        def _(sp):
            for dst, src in ((ct[:], consts), (pt[:], params), (cw[:], conv_w), (dwt[:], dw), (wba_raw[:], w_ba)):
                sp.dma_start(dst, src).then_inc(const_in, 16)
            sp.dma_start(x[:], xt).then_inc(x_in, 16)
            for c in range(RAW):
                sp.dma_start(raw[:, c, :], wts[c]).then_inc(raw_in[c], 16)
            with sp.Fori(1, 4 * G_END // RAW) as i:
                for r in range(RAW):
                    sp.wait_ge(lo_ready, RAW * i + r - RAW + 1)
                    sp.dma_start(raw[:, r, :], wts[RAW * i + r]).then_inc(raw_in[r], 16)

        @block.gpsimd
        def _(pool):
            pool.wait_ge(s["mix_a"], 4)
            for n in range(3):
                src = rows[n:n + 1, :].to_broadcast([P, 8 * P])
                pool.dma_start(xg_space[:, 2 * n:2 * n + 2, :].rearrange("p a b -> p (a b)"), src).then_inc(rows_in, 16)
            pool.dma_start(xg_space[:, 6:8, :].rearrange("p a b -> p (a b)"), w_s).then_inc(rows_in, 16)
            pool.dma_start(x[:], xt).then_inc(x_again, 16)
            for j in range(4):
                pool.wait_ge(out_raw, j + 1)
                pool.dma_start(out[:, CH_K * j:CH_K * j + CH_K, :], conv[:, CH_K * j:CH_K * j + CH_K, :]).then_inc(out_done, 16)
            pool.wait_ge(out_done, 64)

        @block.scalar
        def _(act):
            def copy(dst, src):
                return nc.scalar.activation(dst, src, ACT.Copy)

            def high_part(c, k, turns):
                r = k % RAW
                act.wait_ge(raw_in[r], 16 * (turns + 1))
                act.wait_ge(chunk_free, c + 1)
                nc.scalar.activation(whi[:, r].rearrange("p a b -> p (a b)"), raw[:, r, :], ACT.Copy).then_inc(hi_ready, 1)

            def splits(G):
                for k in range(2, 6):
                    if not (isinstance(G, int) and 4 * G + k >= 4 * G_END):
                        high_part(4 * G + k, k, 2 * G + k // 2)

            def copy_cross(G, par, bias=None):
                act.wait_ge(chunk_free, SPLIT + 4 * G + 4)
                act.wait_ge(banks_free, G + 2)
                src = ps[:, 4 * par:4 * par + 4, T:2 * T]
                if bias is None:
                    copy(cross[:], src).then_inc(cross_ready, 1)
                    return
                for t in range(CH_K):
                    ins = nc.scalar.activation(cross[:, t, :], src[:, t, :], ACT.Identity, bias=bias[:, t:t + 1])
                ins.then_inc(cross_ready, 1)

            def norm_part(e, j, xw):
                if e >= 4:
                    act.wait_ge(x_new, e - 3)
                if e:
                    act.wait_ge(ssum_part, e)
                nc.scalar.activation(padded[:, :, 0:T], xw, ACT.Square).then_inc(sq_ready, 1)
                if j is not None:
                    act.wait_ge(xg_raw, e + 1)
                    copy(xg[:, 4 * j:4 * j + 4, 0, :], total[:]).then_inc(xg_hi, 1)

            def root(n):
                act.wait_ge(ms_ready, n + 1)
                nc.scalar.activation(sq_part[:], ps[:, 7, 0:T], ACT.Sqrt, scale=1.0 / D, bias=eps).then_inc(root_ready, 1)

            eps, eps_q = param("eps"), param("eps_q")
            gate_bias = param("pw1_b")[:, KT:2 * KT]
            high_part(0, 0, 0)
            high_part(1, 1, 0)
            act.wait_ge(const_in, 80)
            act.wait_ge(x_in, 16)
            copy(wba[:, :, 0, :], wba_raw[:]).then_inc(s["wba_hi"], 1)
            for j in range(4):
                norm_part(j, j, x[:, 4 * j:4 * j + 4, :])
            root(0)
            act.wait_ge(s["ba_prod"], 1)
            copy(flat_small[:, 0:32].rearrange("p (m c) -> p m c", m=TT),
                 ps[:, 6, 0:128].rearrange("p (m c) -> p m c", m=TT)[:, :, NB:2 * NB]).then_inc(s["ba_cross"], 1)
            nc.scalar.activation(flat_small[:, 128:130], ps[:, 6, 128:130], ACT.Sqrt, scale=1.0 / D, bias=eps).then_inc(s["ba_cross"], 1)
            act.wait_ge(s["ba_sum"], 1)
            nc.scalar.activation(gates[:, 0], gates[:, 5], ACT.Sigmoid).then_inc(s["beta"], 1)
            nc.scalar.activation(gates[:, 1], gates[:, 6], ACT.Abs).then_inc(act_step, 1)
            act.wait_ge(act_step, 1)
            nc.scalar.activation(gates[:, 2], gates[:, 1], ACT.Exp, scale=-1.0).then_inc(act_step, 1)
            act.wait_ge(act_step, 2)
            nc.scalar.activation(gates[:, 1], gates[:, 2], ACT.Ln, bias=1.0).then_inc(s["softplus"], 1)
            nc.scalar.activation(flat_small[:, 136:144], param("a_log"), ACT.Exp).then_inc(s["softplus"], 1)
            act.wait_ge(s["g"], 2)
            nc.scalar.activation(gates[:, 3], gates[:, 2], ACT.Exp).then_inc(s["gates"], 1)
            nc.scalar.activation(gates[:, 4], gates[:, 4], ACT.Exp).then_inc(s["gates"], 1)

            for G in range(G_QKVZ, G_UV):
                splits(G)
                copy_cross(G, G % 2)
                act.wait_ge(s["qkvz_raw"], G + 1)
                t0 = QKVZ_AT[G]
                nc.scalar.activation(acts[:, t0:t0 + 4, :], acts[:, t0:t0 + 4, :], ACT.Silu).then_inc(s["qkvz_ready"], 1)
            for G in range(G_UV, G_WOUT):
                splits(G)
                copy_cross(G, G % 2)
                act.wait_ge(scaled, G - G_UV + 1)
                i = G - G_UV
                for a, t0 in ((0, 32 + 2 * i), (2, 40 + 2 * i)):
                    ins = nc.scalar.activation(acts[:, t0:t0 + 2, :], total[:, a:a + 2, :], ACT.Gelu)
                ins.then_inc(s["uv_ready"], 1)

            for b in range(4):
                hh, m = b // 2, b % 2
                act.wait_ge(s["tok"], b + 1)
                if b:
                    act.wait_ge(s["mix_a"], b)
                nc.scalar.activation(buf["sq_k"], bank(0), ACT.Square)
                nc.scalar.activation(buf["sq_q"], bank(1), ACT.Square).then_inc(s["tok_sq"], 1)
                act.wait_ge(s["ss"], b + 1)
                nc.scalar.activation(sm(1, 4), sm(0, 4), ACT.Sqrt, bias=eps)
                nc.scalar.activation(sm(1, 8)[:, 4:8], sm(0, 8)[:, 4:8], ACT.Sqrt, scale=float(P), bias=eps_q).then_inc(s["root"], 1)
                act.wait_ge(s["gb"], b + 1)
                nc.scalar.activation(elast, bank(7)[:, :, C - 1::C], ACT.Exp).then_inc(s["elast"], 1)
                act.wait_ge(s["decay_in"], b + 1)
                nc.scalar.activation(buf["decay"], buf["lg"], ACT.Exp).then_inc(s["decay"], 1)
                act.wait_ge(s["feat"], b + 1)
                copy(buf["qnT"], bank(5))
                copy(buf["qdT"], bank(6)).then_inc(s["feat_act"], 1)
                act.wait_ge(s["t_prod"], b + 1)
                copy(buf["T"], bank(2)).then_inc(s["t_copy"], 1)
                for lev in range(1, LEVELS):
                    act.wait_ge(s["ut_prod"], LEVELS * b + lev)
                    copy(buf["T"], bank(5)).then_inc(s["t_copy"], 1)
                act.wait_ge(s["w_prod"], b + 1)
                nc.scalar.activation(buf["wT"], bank(6), ACT.Copy, scale=-1.0).then_inc(s["w_copy"], 1)
                for cc in range(2):
                    R = slice(C * cc, C * cc + C)
                    act.wait_ge(s["v_prod"], 2 * b + cc + 1)
                    copy(buf["v_new"][R], bank(7)[R]).then_inc(s["v_copy"], 1)
                act.wait_ge(s["s_prod"], 2 * b + 2)
                nc.scalar.activation(buf["o_sq"], bank(0), ACT.Square).then_inc(s["o_sq"], 1)
                act.wait_ge(s["o_ss"], b + 1)
                nc.scalar.activation(sm(3, 4), sm(2, 4), ACT.Sqrt, scale=1.0 / P, bias=eps).then_inc(s["o_root"], 1)
                act.wait_ge(s["gated"], b + 1)
                copy(hid[:, 4 * hh:4 * hh + 4, 0, tok(m)], buf["gate_out"]).then_inc(s["mix_hi"], 1)

            for m in range(TT):
                act.wait_ge(s["gv_center"], m + 1)
                nc.scalar.activation(wide["sq"], wide["center"], ACT.Square).then_inc(s["gv_sq"], 1)
                act.wait_ge(s["gv_ss"], m + 1)
                nc.scalar.activation(sm(6), sm(5), ACT.Sqrt, scale=1.0 / P, bias=eps).then_inc(s["gv_root"], 1)
                act.wait_ge(s["gm_out"], m + 1)
                copy(hid[:, 8:16, 0, tok(m)], wide["mixed"]).then_inc(s["gm_hi"], 1)

            act.wait_ge(x_again, 16)
            for j in range(4):
                G = G_WOUT + j
                splits(G)
                copy_cross(G, G % 2)
                norm_part(4 + j, j, x[:, 4 * j:4 * j + 4, :])

            def mlp(base, layer, q, last, last_norm):
                for j in range(4):
                    G = base + 8 * q + j
                    splits(G)
                    copy_cross(G, j % 2)
                    n = 16 * layer + 4 * q + j
                    act.wait_ge(hid_raw, n + 1)
                    copy(hid[:, 4 * j:4 * j + 4, 0, :], padded[:, :, 0:T]).then_inc(hid_hi, 1)
                for j in range(4):
                    G = base + 8 * q + 4 + j
                    splits(G)
                    copy_cross(G, j % 2)
                    if last:
                        e = 8 + 8 * layer + j
                        norm_part(e, j if not last_norm else None, x[:, 4 * j:4 * j + 4, :])

            root(1)
            with act.Fori(0, NQ - 1) as q:
                mlp(G_MLP0, 0, q, False, False)
            mlp(G_MLP0, 0, NQ - 1, True, False)

            root(2)
            with act.Fori(0, 4) as i:
                for par in range(2):
                    G = G_PW1 + 2 * i + par
                    splits(G)
                    copy_cross(G, par)
                    act.wait_ge(s["glu_scaled"], 2 * i + par + 1)
                    for t in range(2):
                        ins = nc.scalar.activation(total[:, 2 + t, :], total[:, 2 + t, :], ACT.Sigmoid,
                                                   bias=gate_bias[:, bass.ds(4 * i + 2 * par + t, 1)])
                    ins.then_inc(s["gate"], 1)
            act.wait_ge(s["ln_center"], 1)
            nc.scalar.activation(zpad[:, :, 0:T], conv, ACT.Square).then_inc(s["ln_sq"], 1)
            act.wait_ge(s["ln_ms"], 1)
            nc.scalar.activation(sq_part[:], ps[:, 7, 0:T], ACT.Sqrt, scale=1.0 / D, bias=eps).then_inc(s["ln_root"], 1)
            for j in range(4):
                act.wait_ge(s["ln_norm"], j + 1)
                for t in range(4 * j, 4 * j + 4):
                    ins = nc.scalar.activation(conv[:, t, :], conv[:, t, :], ACT.Silu, scale=param("ln_g")[:, t:t + 1],
                                               bias=param("ln_b")[:, t:t + 1])
                ins.then_inc(s["ln_act"], 1)
                act.wait_ge(s["ln_act"], j + 1)
                copy(hid[:, 4 * j:4 * j + 4, 0, :], conv[:, 4 * j:4 * j + 4, :]).then_inc(hid_hi, 1)
            for j in range(4):
                G = G_PW2 + j
                splits(G)
                copy_cross(G, G % 2, bias=param("pw2_b")[:, 4 * j:4 * j + 4])
                norm_part(12 + j, j, x[:, 4 * j:4 * j + 4, :])

            root(3)
            with act.Fori(0, NQ - 1) as q:
                mlp(G_MLP1, 1, q, False, False)
            mlp(G_MLP1, 1, NQ - 1, True, True)
            root(4)

        @block.vector
        def _(dve):
            tt = nc.vector.tensor_tensor
            stt = nc.vector.scalar_tensor_tensor
            chain = [0]

            def link(ins):
                chain[0] += 1
                ins.then_inc(dve_step, 1)
                dve.wait_ge(dve_step, chain[0])

            def splits(G):
                for k in range(2, 6):
                    if not (isinstance(G, int) and 4 * G + k >= 4 * G_END):
                        low_part(4 * G + k, k)

            def low_part(c, k):
                r = k % RAW
                dve.wait_ge(hi_ready, c + 1)
                hi = whi[:, r].rearrange("p a b -> p (a b)").bitcast(F32)
                tt(wlo[:, r].rearrange("p a b -> p (a b)"), raw[:, r, :], hi, ALU.subtract).then_inc(lo_ready, 1)

            def leave_psum(G, par):
                dve.wait_ge(cross_ready, G + 1)
                tt(total[:], ps[:, 4 * par:4 * par + 4, 0:T], cross[:], ALU.add).then_inc(banks_free, 1)
                dve.wait_ge(banks_free, G + 3)

            def by_token(ap, n):
                return ap.unsqueeze(1).to_broadcast([P, n, T])

            def norm_part(e, j, gain, first):
                xw = x[:, 4 * j:4 * j + 4, :]
                if gain is not None:
                    g = param(gain)[:, 4 * j:4 * j + 4].unsqueeze(2).to_broadcast([P, 4, T])
                    tt(total[:], xw, g, ALU.mult).then_inc(xg_raw, 1)
                dve.wait_ge(sq_ready, e + 1)
                squares = padded[:, :, 0:T].rearrange("p n t -> p t n")
                nc.vector.tensor_reduce(ssum[:] if first else sq_part[:], squares, AX, ALU.add).then_inc(ssum_part, 1)
                dve.wait_ge(ssum_part, e + 1)
                if j == 3:
                    tt(ssum[:], ssum[:], sq_part[:], ALU.add).then_inc(ssum_ready, 1)
                    dve.wait_ge(ssum_ready, e // 4 + 1)
                elif j:
                    link(tt(ssum[:], ssum[:], sq_part[:], ALU.add))
                if gain is not None:
                    dve.wait_ge(xg_hi, e + 1)
                    tt(xg[:, 4 * j:4 * j + 4, 1, :], total[:], xg[:, 4 * j:4 * j + 4, 0, :].bitcast(F32),
                       ALU.subtract).then_inc(xg_ready, 1)
                    dve.wait_ge(xg_ready, e + 1)

            def rms_of(n):
                dve.wait_ge(root_ready, n + 1)
                nc.vector.reciprocal(rms[:], sq_part[:]).then_inc(rms_ready, 1)
                dve.wait_ge(rms_ready, n + 1)

            low_part(0, 0)
            low_part(1, 1)
            dve.wait_ge(s["wba_hi"], 1)
            tt(wba[:, :, 1, :], wba_raw[:], wba[:, :, 0, :].bitcast(F32), ALU.subtract).then_inc(s["wba_ready"], 1)
            dve.wait_ge(const_in, 80)
            dve.wait_ge(x_in, 16)
            for j in range(4):
                norm_part(j, j, "e_norm", j == 0)
            rms_of(0)
            dve.wait_ge(s["ba_cross"], 2)
            ba = ps[:, 6, 0:128].rearrange("p (m c) -> p m c", m=TT)[:, :, 0:NB]
            crossed = flat_small[:, 0:32].rearrange("p (m c) -> p m c", m=TT)
            both = flat_small[:, 32:64].rearrange("p (m c) -> p m c", m=TT)
            tt(both, ba, crossed, ALU.add)
            link(nc.vector.reciprocal(flat_small[:, 130:132], flat_small[:, 128:130]))
            for m in range(TT):
                nc.vector.tensor_scalar(gates[:, 5, m], both[:, m, 0:H], flat_small[:, 130 + m:131 + m], None, ALU.mult)
                ins = nc.vector.scalar_tensor_tensor(gates[:, 6, m], both[:, m, H:2 * H], flat_small[:, 130 + m:131 + m],
                                                     param("dt_bias"), ALU.mult, ALU.add)
            ins.then_inc(s["ba_sum"], 1)
            dve.wait_ge(s["softplus"], 2)
            link(stt(gates[:, 1], gates[:, 6], 0.0, gates[:, 1], ALU.max, ALU.add))
            stt(gates[:, 1], gates[:, 1], -1.0, flat_small[:, 136:144].unsqueeze(1).to_broadcast([P, TT, H]),
                ALU.mult, ALU.mult).then_inc(s["g"], 1)
            dve.wait_ge(s["gc_prod"], 1)
            link(nc.vector.tensor_copy(gates[:, 2], ps[:, 6, 0:16].rearrange("p (m h) -> p m h", m=TT)))
            tt(gates[:, 4], ps[:, 6, 16:32].rearrange("p (m h) -> p m h", m=TT), gates[:, 2], ALU.subtract).then_inc(s["g"], 1)

            link(nc.vector.memset(padded[:, :, 0:3], 0.0))
            for G in range(G_QKVZ, G_UV):
                splits(G)
                leave_psum(G, G % 2)
                t0 = QKVZ_AT[G]
                if G >= 6:
                    tt(acts[:, t0:t0 + 4, :], total[:], by_token(rms[:], 4), ALU.mult).then_inc(s["qkvz_raw"], 1)
                    continue
                link(tt(padded[:, :, 3:3 + T], total[:], by_token(rms[:], 4), ALU.mult))
                for k in range(4):
                    for t in range(4):
                        w = cw[:, t0 + t, k:k + 1]
                        dst, src = acts[:, t0 + t, :], padded[:, t, k:k + T]
                        if k == 0:
                            ins = nc.vector.tensor_scalar(dst, src, w, None, ALU.mult)
                        else:
                            ins = stt(dst, src, w, dst, ALU.mult, ALU.add)
                    if k < 3:
                        link(ins)
                ins.then_inc(s["qkvz_raw"], 1)
            for G in range(G_UV, G_WOUT):
                splits(G)
                if G > G_UV:
                    dve.wait_ge(s["uv_ready"], G - G_UV)
                leave_psum(G, G % 2)
                tt(total[:], total[:], by_token(rms[:], 4), ALU.mult).then_inc(scaled, 1)

            for b in range(4):
                hh, m = b // 2, b % 2
                heads = slice(HH * hh, HH * hh + HH)
                beta, g, gc, eg, et = (gates[:, i, m, heads] for i in range(5))
                if b == 0:
                    dve.wait_ge(chunk_free, SPLIT + 4 * G_WOUT)
                    dve.wait_ge(s["gates"], 2)
                tt(buf["lg"], all_heads(const("upto")), per_head(g), ALU.mult).then_inc(s["lg"], 1)
                dve.wait_ge(s["tok_sq"], b + 1)
                nc.vector.tensor_reduce(sm(0, 4), buf["sq_k"], AX, ALU.add)
                nc.vector.tensor_reduce(sm(0, 8)[:, 4:8], buf["sq_q"], AX, ALU.add).then_inc(s["ss"], 1)
                dve.wait_ge(s["root"], b + 1)
                link(nc.vector.reciprocal(sm(4), sm(1)))
                tt(buf["kn"], bank(0), per_head(sm(4, 4)), ALU.mult)
                tt(buf["qn"], bank(1), per_head(sm(4, 8)[:, 4:8]), ALU.mult)
                link(tt(buf["vb"], bank(2), per_head(beta), ALU.mult))
                tt(buf["kt"], buf["kn"], per_head(et), ALU.mult)
                tt(buf["qd"], buf["qn"], per_head(eg), ALU.mult)
                tt(buf["kb"], buf["kn"], per_head(beta), ALU.mult).then_inc(s["normed"], 1)
                dve.wait_ge(s["elast"], b + 1)
                link(tt(buf["lg"], bank(7), per_head(gc), ALU.subtract))
                tt(buf["lg"], buf["lg"], all_heads(const("fill")), ALU.min).then_inc(s["decay_in"], 1)
                tt(buf["kd"], buf["kb"], per_head(eg), ALU.mult)
                dve.wait_ge(s["feat"], b + 1)
                nc.vector.tensor_copy(buf["knT"], bank(3))
                nc.vector.tensor_copy(buf["kbT"], bank(4)).then_inc(s["feat_dve"], 1)
                dve.wait_ge(s["decay"], b + 1)
                link(tt(buf["decay_s"], buf["decay"], all_heads(const("strict")), ALU.mult))
                dve.wait_ge(s["prods"], b + 1)
                tt(buf["attnT"], bank(1), buf["decay"], ALU.mult)
                link(tt(buf["C"], bank(0), buf["decay_s"], ALU.mult))
                link(tt(buf["C"], buf["C"], all_heads(const("ident")), ALU.add))
                tt(buf["U"], buf["C"], all_heads(const("lev0t")), ALU.mult).then_inc(s["inv0"], 1)
                for lev in range(1, LEVELS + 1):
                    dve.wait_ge(s["y_prod"], LEVELS * b + lev)
                    tt(buf["Z"], bank(3), all_heads(const(f"lev{lev}")), ALU.mult).then_inc(s["z"], 1)
                    dve.wait_ge(s["ut_prod"], LEVELS * b + lev)
                    nc.vector.tensor_copy(buf["U"], bank(4)).then_inc(s["u_copy"], 1)
                if m == 0:
                    nc.vector.memset(buf["state"], 0.0).then_inc(s["state"], 1)
                for cc in range(2):
                    if m == 0 or cc == 1:
                        dve.wait_ge(s["state"], 5 * hh + 2 * m + cc + 1)
                    link(tt(buf["state_d"], buf["state"], elast[:, :, cc].unsqueeze(2).to_broadcast([P, HH, P]), ALU.mult))
                    dve.wait_ge(s["s_prod"], 2 * b + cc + 1)
                    tt(buf["state"], bank(1), buf["state_d"], ALU.add).then_inc(s["state"], 1)
                dve.wait_ge(s["o_sq"], b + 1)
                nc.vector.tensor_reduce(sm(2, 4), buf["o_sq"], AX, ALU.add).then_inc(s["o_ss"], 1)
                dve.wait_ge(s["o_root"], b + 1)
                link(nc.vector.reciprocal(sm(7, 4), sm(3, 4)))
                tt(buf["o_n"], bank(0), per_head(sm(7, 4)), ALU.mult).then_inc(s["o_norm"], 1)
                dve.wait_ge(s["o_prod"], b + 1)
                z0 = 24 + HH * hh
                stt(buf["gate_out"], bank(2), param("head_norm"), acts[:, z0:z0 + HH, tok(m)], ALU.mult,
                    ALU.mult).then_inc(s["gated"], 1)
                dve.wait_ge(s["mix_hi"], b + 1)
                dst = hid[:, HH * hh:HH * hh + HH, :, tok(m)]
                tt(dst[:, :, 1, :], buf["gate_out"], dst[:, :, 0, :].bitcast(F32), ALU.subtract).then_inc(s["mix_a"], 1)

            for m in range(TT):
                if m == 0:
                    dve.wait_ge(rows_in, 64)
                    nc.vector.memset(wide["w_s"][C:P, :, 0:C], 0.0)
                dve.wait_ge(s["gv_prod"], m + 1)
                wide_of = lambda ap: ap.unsqueeze(2).to_broadcast([P, 8, P])
                link(nc.vector.tensor_reduce(sm(8), pair(0), AX, ALU.add))
                link(nc.vector.tensor_scalar(sm(8), sm(8), 1.0 / P, None, ALU.mult))
                tt(wide["center"], pair(0), wide_of(sm(8)), ALU.subtract).then_inc(s["gv_center"], 1)
                dve.wait_ge(s["gv_sq"], m + 1)
                nc.vector.tensor_reduce(sm(5), wide["sq"], AX, ALU.add).then_inc(s["gv_ss"], 1)
                dve.wait_ge(s["gv_root"], m + 1)
                link(nc.vector.reciprocal(sm(4), sm(6)))
                link(tt(wide["center"], wide["center"], wide_of(sm(4)), ALU.mult))
                link(tt(wide["center"], wide["center"], wide["ln_g"], ALU.mult))
                tt(wide["center"], wide["center"], wide["ln_b"], ALU.add).then_inc(s["gv_norm"], 1)
                dve.wait_ge(s["mixed"], m + 1)
                link(tt(wide["mixed"], pair(2), wide["b_s"], ALU.add))
                tt(wide["mixed"], wide["mixed"], acts[:, 32:40, tok(m)], ALU.mult).then_inc(s["gm_out"], 1)
                dve.wait_ge(s["gm_hi"], m + 1)
                dst = hid[:, 8:16, :, tok(m)]
                tt(dst[:, :, 1, :], wide["mixed"], dst[:, :, 0, :].bitcast(F32), ALU.subtract).then_inc(s["mix_b"], 1)

            dve.wait_ge(x_again, 16)

            def onto_residual(G, par, j, e, gain, part=0):
                leave_psum(G, par)
                ins = tt(x[:, 4 * j:4 * j + 4, :], x[:, 4 * j:4 * j + 4, :], total[:], ALU.add)
                if e is not None:
                    ins.then_inc(x_new, 1)
                    dve.wait_ge(x_new, e - 3)
                    norm_part(e, j, gain, j == 0)
                else:
                    ins.then_inc(x_part, 1)
                    dve.wait_ge(x_part, part + 1)

            for j in range(4):
                splits(G_WOUT + j)
                onto_residual(G_WOUT + j, j % 2, j, 4 + j, "f_norm0")

            def mlp(base, layer, q, last, gain):
                for j in range(4):
                    G = base + 8 * q + j
                    n = 16 * layer + 4 * q + j
                    splits(G)
                    leave_psum(G, j % 2)
                    tt(total[:], total[:], by_token(rms[:], 4), ALU.mult).then_inc(hid_scaled, 1)
                    dve.wait_ge(hid_scaled, n + 1)
                    stt(padded[:, :, 0:T], total[:], 0.0, total[:], ALU.max, ALU.mult).then_inc(hid_raw, 1)
                    dve.wait_ge(hid_hi, n + 4 * layer + 1)
                    tt(hid[:, 4 * j:4 * j + 4, 1, :], padded[:, :, 0:T], hid[:, 4 * j:4 * j + 4, 0, :].bitcast(F32),
                       ALU.subtract).then_inc(hid_ready, 1)
                    dve.wait_ge(hid_ready, n + 4 * layer + 1)
                for j in range(4):
                    G = base + 8 * q + 4 + j
                    splits(G)
                    onto_residual(G, j % 2, j, 8 + 8 * layer + j if last else None, gain, 12 * layer + 4 * q + j)

            rms_of(1)
            with dve.Fori(0, NQ - 1) as q:
                mlp(G_MLP0, 0, q, False, None)
            mlp(G_MLP0, 0, NQ - 1, True, "o_norm")

            rms_of(2)
            nc.vector.memset(zpad[:, :, 0:32], 0.0)
            before = chain[0]
            with dve.Fori(0, 4) as i:
                for par in range(2):
                    G = G_PW1 + 2 * i + par
                    splits(G)
                    leave_psum(G, par)
                    tt(total[:], total[:], by_token(rms[:], 4), ALU.mult).then_inc(s["glu_scaled"], 1)
                    dve.wait_ge(s["gate"], 2 * i + par + 1)
                    tile0 = 4 * i + 2 * par
                    for t in range(2):
                        ins = stt(zpad[:, bass.ds(tile0 + t, 1), 32:32 + T].rearrange("p a t -> p (a t)"), total[:, t, :],
                                  param("pw1_b")[:, bass.ds(tile0 + t, 1)], total[:, 2 + t, :], ALU.add, ALU.mult)
                    ins.then_inc(s["glu"], 1)
                    dve.wait_ge(s["glu"], 2 * i + par + 1)
                    for k in range(WD):
                        for t in range(2):
                            src = zpad[:, bass.ds(tile0 + t, 1), 2 + k:2 + k + T].rearrange("p a t -> p (a t)")
                            dst = conv[:, bass.ds(tile0 + t, 1), :].rearrange("p a t -> p (a t)")
                            w = dwt[:, bass.ds(tile0 + t, 1), k:k + 1].rearrange("p a t -> p (a t)")
                            if k == 0:
                                ins = nc.vector.tensor_scalar(dst, src, w, param("dw_b")[:, bass.ds(tile0 + t, 1)],
                                                              ALU.mult, ALU.add)
                            else:
                                ins = stt(dst, src, w, dst, ALU.mult, ALU.add)
                        ins.then_inc(s["tap"], 1)
                        dve.wait_ge(s["tap"], 2 * WD * i + WD * par + k + 1)
            chain[0] = before
            nc.vector.tensor_reduce(ssum[:], conv.rearrange("p n t -> p t n"), AX, ALU.add).then_inc(s["ln_sum"], 1)
            dve.wait_ge(s["ln_mean"], 1)
            link(nc.vector.tensor_scalar(rms[:], ps[:, 7, 0:T], 1.0 / D, None, ALU.mult))
            tt(conv, conv, by_token(rms[:], KT), ALU.subtract).then_inc(s["ln_center"], 1)
            dve.wait_ge(s["ln_sq"], 1)
            nc.vector.tensor_reduce(ssum[:], zpad[:, :, 0:T].rearrange("p n t -> p t n"), AX, ALU.add).then_inc(s["ln_ss"], 1)
            dve.wait_ge(s["ln_root"], 1)
            link(nc.vector.reciprocal(rms[:], sq_part[:]))
            for j in range(4):
                w = conv[:, 4 * j:4 * j + 4, :]
                tt(w, w, by_token(rms[:], 4), ALU.mult).then_inc(s["ln_norm"], 1)
            for j in range(4):
                dve.wait_ge(hid_hi, 17 + j)
                tt(hid[:, 4 * j:4 * j + 4, 1, :], conv[:, 4 * j:4 * j + 4, :], hid[:, 4 * j:4 * j + 4, 0, :].bitcast(F32),
                   ALU.subtract).then_inc(hid_ready, 1)
            for j in range(4):
                splits(G_PW2 + j)
                onto_residual(G_PW2 + j, j % 2, j, 12 + j, "f_norm1")

            rms_of(3)
            with dve.Fori(0, NQ - 1) as q:
                mlp(G_MLP1, 1, q, False, None)
            mlp(G_MLP1, 1, NQ - 1, True, None)
            rms_of(4)
            for j in range(4):
                w = conv[:, 4 * j:4 * j + 4, :]
                g = param("final_norm")[:, 4 * j:4 * j + 4].unsqueeze(2).to_broadcast([P, 4, T])
                link(tt(w, x[:, 4 * j:4 * j + 4, :], by_token(rms[:], 4), ALU.mult))
                tt(w, w, g, ALU.mult).then_inc(out_raw, 1)

        @block.tensor
        def _(pe):
            mm = nc.tensor.matmul

            def group(G, par, operand, ready, counts):
                pe.wait_ge(banks_free, G + 1)
                for kc in range(4):
                    pe.wait_ge(lo_ready, 4 * G + kc + 1)
                    if ready is not None:
                        pe.wait_ge(ready, counts + kc)
                    r = kc % SPLIT
                    for k in range(CH_K):
                        kt = CH_K * kc + k
                        for n in range(4):
                            cols = slice(P * n, P * n + P)
                            mm(ps[:, 4 * par + n, :], whi[:, r, k, cols], operand[:, kt].rearrange("p a t -> p (a t)"),
                               start=(kt == 0), stop=False)
                            ins = mm(ps[:, 4 * par + n, T:2 * T], wlo[:, r, k, cols], operand[:, kt, 0, :],
                                     start=False, stop=(kt == KT - 1))
                    ins.then_inc(chunk_free, 1)

            def mean_squares(n):
                pe.wait_ge(ssum_ready, n + 1)
                mm(ps[:, 7, 0:T], const("ones"), ssum[:], start=True, stop=True).then_inc(ms_ready, 1)

            pe.sem_inc(chunk_free, SPLIT)
            pe.sem_inc(banks_free, 2)
            mean_squares(0)
            pe.wait_ge(s["wba_ready"], 1)
            pe.wait_ge(xg_ready, 4)
            for m in range(TT):
                for kt in range(KT):
                    mm(ps[:, 6, 64 * m:64 * m + 2 * NB], xg[:, kt, 0, tok(m)], wba[:, kt].rearrange("p a b -> p (a b)"),
                       start=(kt == 0), stop=False)
                    mm(ps[:, 6, 64 * m + NB:64 * m + 2 * NB], xg[:, kt, 1, tok(m)], wba[:, kt, 0, :],
                       start=False, stop=(kt == KT - 1))
            for m in range(TT):
                ins = mm(ps[:, 6, 128 + m:129 + m], ssum[:, tok(m)], const("ones")[:, 0:1], start=True, stop=True)
            ins.then_inc(s["ba_prod"], 1)
            pe.wait_ge(s["g"], 1)
            mm(ps[:, 6, 0:16], const("upto"), gates[:, 1].rearrange("p m h -> p (m h)"), start=True, stop=True)
            mm(ps[:, 6, 16:32], const("chunk"), gates[:, 1].rearrange("p m h -> p (m h)"), start=True,
               stop=True).then_inc(s["gc_prod"], 1)
            pe.wait_ge(s["gates"], 2)
            pe.wait_ge(root_ready, 1)
            with pe.Fori(0, G_WOUT // 2) as i:
                for par in range(2):
                    group(2 * i + par, par, xg, None, 0)

            def transposes(b, src):
                for h in range(HH):
                    ins = nc.tensor.transpose(bank(b)[:, h, :], src(h), const("ident"))
                return ins

            def products(b, left, right):
                for h in range(HH):
                    ins = mm(bank(b)[:, h, :], left[:, h, :], right[:, h, :], start=True, stop=True)
                return ins

            pe.wait_ge(banks_free, 2 + G_WOUT)
            pe.wait_ge(s["qkvz_ready"], 8)
            for b in range(4):
                hh, m = b // 2, b % 2
                if b:
                    pe.wait_ge(s["gated"], b)
                transposes(0, lambda h: acts[:, 8 + HH * hh + h, tok(m)])
                transposes(1, lambda h: acts[:, HH * hh + h, tok(m)])
                transposes(2, lambda h: acts[:, 16 + HH * hh + h, tok(m)]).then_inc(s["tok"], 1)
                pe.wait_ge(s["lg"], b + 1)
                mm(ps[:, 7, :], const("ones"), buf["lg"].rearrange("p h c -> p (h c)"), start=True, stop=True).then_inc(s["gb"], 1)
                pe.wait_ge(s["normed"], b + 1)
                transposes(3, lambda h: buf["kn"][:, h, :])
                transposes(4, lambda h: buf["kb"][:, h, :])
                transposes(5, lambda h: buf["qn"][:, h, :])
                transposes(6, lambda h: buf["qd"][:, h, :]).then_inc(s["feat"], 1)
                pe.wait_ge(s["feat_dve"], b + 1)
                pe.wait_ge(s["feat_act"], b + 1)
                products(0, buf["knT"], buf["kbT"])
                products(1, buf["knT"], buf["qnT"]).then_inc(s["prods"], 1)
                pe.wait_ge(s["inv0"], b + 1)
                transposes(2, lambda h: buf["U"][:, h, :]).then_inc(s["t_prod"], 1)
                for lev in range(1, LEVELS + 1):
                    pe.wait_ge(s["t_copy"], LEVELS * b + lev)
                    if lev > 1:
                        pe.wait_ge(s["u_copy"], LEVELS * b + lev - 1)
                    products(3, buf["C"], buf["T"]).then_inc(s["y_prod"], 1)
                    pe.wait_ge(s["z"], LEVELS * b + lev)
                    ins = products(4, buf["Z"], buf["U"])
                    if lev < LEVELS:
                        ins = products(5, buf["U"], buf["Z"])
                    ins.then_inc(s["ut_prod"], 1)
                pe.wait_ge(s["u_copy"], LEVELS * b + LEVELS)
                products(6, buf["kd"], buf["U"]).then_inc(s["w_prod"], 1)
                pe.wait_ge(s["w_copy"], b + 1)
                for cc in range(2):
                    R = slice(C * cc, C * cc + C)
                    pe.wait_ge(s["state"], 5 * hh + 2 * m + cc + 1)
                    for h in range(HH):
                        mm(bank(7)[R, h, :], buf["U"][:, h, R], buf["vb"][:, h, :], start=True, stop=False)
                        ins = mm(bank(7)[R, h, :], buf["wT"][:, h, R], buf["state"][:, h, :], start=False, stop=True)
                    ins.then_inc(s["v_prod"], 1)
                    pe.wait_ge(s["v_copy"], 2 * b + cc + 1)
                    for h in range(HH):
                        mm(bank(0)[R, h, :], buf["qdT"][:, h, R], buf["state"][:, h, :], start=True, stop=False)
                        mm(bank(0)[R, h, :], buf["attnT"][R, h, R], buf["v_new"][R, h, :], start=False, stop=True)
                    for h in range(HH):
                        ins = mm(bank(1)[:, h, :], buf["kt"][R, h, :], buf["v_new"][R, h, :], start=True, stop=True)
                    ins.then_inc(s["s_prod"], 1)
                pe.wait_ge(s["o_norm"], b + 1)
                transposes(2, lambda h: buf["o_n"][:, h, :]).then_inc(s["o_prod"], 1)

            for m in range(TT):
                if m == 0:
                    pe.wait_ge(s["mix_a"], 4)
                    pe.wait_ge(s["uv_ready"], 4)
                else:
                    pe.wait_ge(s["gv_center"], m)
                for g in range(8):
                    ins = nc.tensor.transpose(pair(0)[:, g, :], acts[:, 40 + g, tok(m)], const("ident"))
                ins.then_inc(s["gv_prod"], 1)
                pe.wait_ge(s["gv_norm"], m + 1)
                for g in range(8):
                    ins = mm(pair(2)[:, g, :], wide["center"][:, g, :], wide["w_s"][:, g, :], start=True, stop=True)
                ins.then_inc(s["mixed"], 1)

            pe.wait_ge(s["mix_b"], 2)
            with pe.Fori(0, 2) as i:
                for par in range(2):
                    group(G_WOUT + 2 * i + par, par, hid, None, 0)

            def mlp(base, layer):
                mean_squares(1 + 2 * layer)
                pe.wait_ge(root_ready, 2 + 2 * layer)
                with pe.Fori(0, NQ) as q:
                    with pe.Fori(0, 2) as i:
                        for par in range(2):
                            group(base + 8 * q + 2 * i + par, par, xg, xg_ready, 4 + 8 * layer + 1)
                    with pe.Fori(0, 2) as i:
                        for par in range(2):
                            group(base + 8 * q + 4 + 2 * i + par, par, hid, hid_ready, 20 * layer + 4 * q + 1)

            mlp(G_MLP0, 0)
            mean_squares(2)
            pe.wait_ge(root_ready, 3)
            with pe.Fori(0, 4) as i:
                for par in range(2):
                    group(G_PW1 + 2 * i + par, par, xg, xg_ready, 9)
            pe.wait_ge(s["ln_sum"], 1)
            mm(ps[:, 7, 0:T], const("ones"), ssum[:], start=True, stop=True).then_inc(s["ln_mean"], 1)
            pe.wait_ge(s["ln_ss"], 1)
            mm(ps[:, 7, 0:T], const("ones"), ssum[:], start=True, stop=True).then_inc(s["ln_ms"], 1)
            pe.wait_ge(s["ln_root"], 1)
            with pe.Fori(0, 2) as i:
                for par in range(2):
                    group(G_PW2 + 2 * i + par, par, hid, hid_ready, 17)
            mlp(G_MLP1, 1)
            mean_squares(4)


_INS = ["xt", "wts", "w_ba", "consts", "params", "conv_w", "dw", "rows", "w_s"]


def tables():
    import numpy as np
    i = np.arange(P)
    same = i[:, None] // C == i[None, :] // C
    upto = same & (i[:, None] <= i[None, :])
    t = {"ident": np.eye(P), "ones": np.ones((P, P)), "upto": upto, "chunk": same,
         "fill": np.where(upto, 3e38, -3e38), "strict": upto & (i[:, None] < i[None, :])}
    for lev in range(LEVELS + 1):
        size = 1 << lev
        below = (i[:, None] // (2 * size) == i[None, :] // (2 * size)) & (i[:, None] // size > i[None, :] // size)
        m = np.eye(P) - below
        t["lev0t" if lev == 0 else f"lev{lev}"] = m.T if lev == 0 else m
    return np.ascontiguousarray(np.stack([t[n] for n in CONSTS], 1).astype(np.float32))


def kernel(**inputs):
    import numpy as np
    import concourse.bacc as bacc
    from concourse.bass_utils import run_bass_kernel_spmd as run

    a = {n: np.asarray(v) for n, v in inputs.items()}

    def chunks(w):
        w = w.reshape(4, CH_K, P, -1, CH_N)
        return w.transpose(3, 0, 2, 1, 4).reshape(-1, P, CH)

    def tiles(v):
        return v.reshape(-1, P).T

    w_in = a["e_w_in"][0]
    hd = H * P
    q, k, v, z = (w_in[:, i * hd:(i + 1) * hd] for i in range(4))
    ba = w_in[:, 4 * hd:4 * hd + NB]
    u, vr = (w_in[:, 4 * hd + NB + i * hd:4 * hd + NB + (i + 1) * hd] for i in range(2))
    half = CH_N
    cols = [q[:, :half], k[:, :half], v[:, :half], q[:, half:], k[:, half:], v[:, half:], z]
    for i in range(4):
        cols += [u[:, 256 * i:256 * i + 256], vr[:, 256 * i:256 * i + 256]]
    parts = [chunks(np.concatenate(cols, 1)), chunks(a["e_w_out"][0])]

    def mlp(layer):
        for i in range(NQ):
            parts.append(chunks(a["f_w1"][layer][:, i * D:(i + 1) * D]))
            parts.append(chunks(a["f_w2"][layer][i * D:(i + 1) * D]))

    mlp(0)
    pw1 = a["o_pw1"][0]
    cols = []
    for i in range(8):
        cols += [pw1[:, 256 * i:256 * i + 256], pw1[:, D + 256 * i:D + 256 * i + 256]]
    parts += [chunks(np.concatenate(cols, 1)), chunks(a["o_pw2"][0])]
    mlp(1)
    wide = lambda v: np.broadcast_to(v[None, :], (P, v.size))
    params = {"e_norm": tiles(a["e_norm"][0]), "f_norm0": tiles(a["f_norm"][0]), "o_norm": tiles(a["o_norm"][0]),
              "f_norm1": tiles(a["f_norm"][1]), "final_norm": tiles(a["final_norm"]), "pw1_b": tiles(a["o_pw1_b"][0]),
              "dw_b": tiles(a["o_dw_b"][0]), "ln_g": tiles(a["o_ln_g"][0]), "ln_b": tiles(a["o_ln_b"][0]),
              "pw2_b": tiles(a["o_pw2_b"][0]), "head_norm": tiles(a["e_o_norm"][0]), "a_log": wide(a["e_a_log"][0]),
              "dt_bias": wide(a["e_dt_bias"][0]), "eps": np.full((P, 1), EPS, np.float32),
              "eps_q": np.full((P, 1), EPS * P, np.float32)}
    arrays = {
        "xt": a["x"][0].T.reshape(KT, P, T).transpose(1, 0, 2),
        "wts": np.concatenate(parts, 0),
        "w_ba": ba.reshape(KT, P, NB).transpose(1, 0, 2),
        "consts": tables(),
        "params": np.concatenate([params[n] for n in PARAMS], 1),
        "conv_w": a["e_conv_w"][0].reshape(4, 24, P).transpose(2, 1, 0),
        "dw": a["o_dw"][0].reshape(WD, KT, P).transpose(2, 1, 0),
        "rows": np.stack([a["e_ln_g"][0], a["e_ln_b"][0], a["e_b_s"][0].reshape(-1)]),
        "w_s": a["e_w_s"][0].transpose(2, 0, 1).reshape(P, 8 * P),
    }
    arrays = {n: np.ascontiguousarray(v) for n, v in arrays.items()}
    nc = bacc.Bacc("TRN2", target_bir_lowering=False, num_devices=1)
    args = [nc.dram_tensor(f"in_{n}", arrays[n].shape, F32, kind="ExternalInput").ap() for n in _INS]
    out = nc.dram_tensor("out_t", (P, KT, T), F32, kind="ExternalOutput").ap()
    build(nc, *args, out)
    r = run(nc, [{f"in_{n}": v for n, v in arrays.items()}], core_ids=[0])
    return r.results[0]["out_t"].transpose(1, 0, 2).reshape(1, D, T).transpose(0, 2, 1)
```

```python
from contextlib import ExitStack

import concourse.bass as bass
from concourse import mybir
from concourse.alu_op_type import AluOpType as ALU

F32 = mybir.dt.float32
F32R = mybir.dt.float32r
ACT = mybir.ActivationFunctionType
AX = mybir.AxisListType.X

P = 128
D = 2048
T = 256
KT = D // P
TT = T // P
H = 8
HH = 4
C = 64
NQ = 4
NB = 16
WD = 31
CH_K = 4
CH_N = 512
CH = CH_K * CH_N
RAW = 2
HALF = CH // 2
SPLIT = 4
G_QKVZ, G_UV, G_WOUT, G_MLP0, G_PW1, G_PW2, G_MLP1, G_END = 0, 8, 12, 16, 48, 56, 60, 92
UNSPLIT = G_PW2 - G_PW1
EPS = 1e-6
QKVZ_AT = [0, 8, 16, 4, 12, 20, 24, 28]
LEVELS = 5

CONSTS = ["ident", "ones", "upto", "chunk", "fill", "strict", "lev0t"] + [f"lev{i}" for i in range(1, LEVELS + 1)]
PARAMS, _at = {}, 0
for _n, _w in (("e_norm", KT), ("f_norm0", KT), ("o_norm", KT), ("f_norm1", KT), ("final_norm", KT),
               ("pw1_b", 2 * KT), ("dw_b", KT), ("ln_g", KT), ("ln_b", KT), ("pw2_b", KT),
               ("head_norm", 1), ("a_log", H), ("dt_bias", H), ("eps", 1), ("eps_q", 1)):
    PARAMS[_n] = (_at, _at + _w)
    _at += _w
N_PARAMS = _at


def splits_on(G, k):
    if not isinstance(G, int):
        return True
    half = 8 * G + 11 + k
    return half < 8 * G_PW1 or 8 * G_PW2 <= half < 8 * G_END and G >= G_PW2


def build(nc, xt, wts, w_ba, consts, params, conv_w, dw, rows, w_s, out):
    with ExitStack() as ctx:
        def sb(name, shape, dt=F32):
            return ctx.enter_context(nc.sbuf_tensor(name, shape, dt))

        def sem(name):
            return ctx.enter_context(nc.semaphore(name))

        used = (nc.sbuf_base + 63) // 64 * 64
        sb("arena", [P, 8192 + 4096 + 32])
        xg = nc.alloc_sbuf_tensor_at("xg", [P, KT, 2, T], F32R, offset=used)
        xg_space = nc.alloc_sbuf_tensor_at("xg_space", [P, 16, 512], F32, offset=used)
        x = nc.alloc_sbuf_tensor_at("x", [P, KT, T], F32, offset=used + 32768)
        x_space = nc.alloc_sbuf_tensor_at("x_space", [P, 8, 512], F32, offset=used + 32768)
        hid = sb("hid", [P, KT, 2, T], F32R)
        raw = sb("raw", [P, RAW, CH])
        whi = sb("whi", [P, SPLIT, CH_K // 2, CH_N], F32R)
        wlo = sb("wlo", [P, SPLIT, CH_K // 2, CH_N], F32R)
        work = sb("work", [P, 12288])
        cross = sb("cross", [P, CH_K, T])
        total = sb("total", [P, CH_K, T])
        padded = sb("padded", [P, CH_K, T + 4])
        ct = sb("ct", [P, len(CONSTS), P])
        pt = sb("pt", [P, N_PARAMS])
        cw = sb("cw", [P, 24, 4])
        dwt = sb("dwt", [P, KT, WD])
        rms = sb("rms", [P, T])
        ssum = sb("ssum", [P, T])
        sq_part = sb("sq_part", [P, T])
        wba_raw = sb("wba_raw", [P, KT, NB])
        wba = sb("wba", [P, KT, 2, NB], F32R)
        gates = sb("gates", [P, 8, TT, H])
        small = sb("small", [P, 16, TT, H])
        ps = ctx.enter_context(nc.psum_tensor("ps", [P, 8, 512], F32))

        def const(name):
            return ct[:, CONSTS.index(name), :]

        def param(name):
            a, b = PARAMS[name]
            return pt[:, a:b]

        acts = work[:].rearrange("p (n t) -> p n t", t=T)
        conv = work[:, 0:KT * T].rearrange("p (n t) -> p n t", t=T)
        xf = work[:, KT * T:2 * KT * T].rearrange("p (n t) -> p n t", t=T)
        zwin = work[:, 2 * KT * T:2 * KT * T + 4 * (T + 32)].rearrange("p (n t) -> p n t", t=T + 32)

        def bank(b):
            return ps[:, b, :].rearrange("p (h c) -> p h c", h=HH)

        def per_head(ap):
            return ap.unsqueeze(2).to_broadcast([P, HH, P])

        def all_heads(ap):
            return ap.unsqueeze(1).to_broadcast([P, HH, P])

        raw_in = [sem(f"raw_in{i}") for i in range(RAW)]
        const_in, x_in, rows_in, x_again = sem("const_in"), sem("x_in"), sem("rows_in"), sem("x_again")
        hi_ready, lo_ready = sem("hi_ready"), sem("lo_ready")
        raw_used = sem("raw_used")
        half_free = sem("half_free")
        cross_ready = sem("cross_ready")
        banks_free = sem("banks_free")
        hid_scaled = sem("hid_scaled")
        xg_raw, xg_hi, xg_ready = sem("xg_raw"), sem("xg_hi"), sem("xg_ready")
        hid_raw, hid_hi, hid_ready = sem("hid_raw"), sem("hid_hi"), sem("hid_ready")
        x_part = sem("x_part")
        x_new = sem("x_new")
        sq_ready, ssum_part, ssum_ready = sem("sq_ready"), sem("ssum_part"), sem("ssum_ready")
        ms_ready, root_ready, rms_ready = sem("ms_ready"), sem("root_ready"), sem("rms_ready")
        scaled, out_raw, out_done = sem("scaled"), sem("out_raw"), sem("out_done")
        dve_step, act_step = sem("dve_step"), sem("act_step")
        names = ["wba_hi", "wba_ready", "ba_prod", "ba_cross", "ba_sum", "beta", "softplus", "g", "gc_prod", "gates",
                 "qkvz_raw", "qkvz_ready", "uv_ready",
                 "lg", "elast", "tok", "tok_sq", "ss", "root", "normed", "gb", "decay_in", "decay", "feat", "feat_dve", "feat_act",
                 "prods", "inv0", "t_prod", "t_copy", "y_prod", "z", "ut_prod", "u_copy", "w_prod", "w_copy", "state",
                 "v_prod", "v_copy", "s_prod", "o_sq", "o_ss", "o_root", "o_norm", "o_prod", "gated", "mix_hi", "mix_a",
                 "gv_prod", "gv_center", "gv_sq", "gv_ss", "gv_root", "gv_norm", "mixed", "gm_out", "gm_hi", "mix_b",
                 "glu_scaled", "gate", "taps0", "taps1", "ln_sum", "ln_mean", "ln_mu", "ln_center", "ln_sq", "ln_ss", "ln_ms",
                 "ln_root", "ln_rs", "ln_norm", "ln_act"]
        s = {n: sem(n) for n in names}
        block = ctx.enter_context(nc.Block())

        slots = [x_space[:, i, :] for i in range(8)] + [xg_space[:, i, :] for i in range(16)]
        buf = {n: slots[i].rearrange("p (h c) -> p h c", h=HH) for i, n in enumerate(
            ["lg", "kn", "qn", "vb", "kb", "kd", "kt", "qd", "knT", "kbT", "qnT", "qdT", "decay", "decay_s", "attnT",
             "C", "U", "T", "Z", "v_new", "state", "state_d"])}
        buf |= {"sq_k": buf["Z"], "sq_q": buf["T"], "o_n": buf["kn"], "gate_out": buf["qn"], "wT": buf["knT"],
                "o_sq": buf["kb"]}
        wide = {n: xg_space[:, 2 * i:2 * i + 2, :].rearrange("p b (g c) -> p (b g) c", g=HH) for i, n in enumerate(
            ["ln_g", "ln_b", "b_s", "w_s", "center", "sq", "mixed"])}
        elast = small[:, 0:4].rearrange("p a m h -> p (a m h)")[:, 0:8].rearrange("p (h c) -> p h c", c=2)
        flat_small = small[:].rearrange("p a m h -> p (a m h)")

        def sm(i, n=8):
            return flat_small[:, 16 + 8 * i:16 + 8 * i + n]

        def pair(b):
            return ps[:, b:b + 2, :].rearrange("p b (g c) -> p (b g) c", g=HH)

        def tok(m):
            return slice(P * m, P * m + P)

        @block.sync
        def _(sp):
            for dst, src in ((ct[:], consts), (pt[:], params), (cw[:], conv_w), (dwt[:], dw), (wba_raw[:], w_ba)):
                sp.dma_start(dst, src).then_inc(const_in, 16)
            sp.dma_start(x[:], xt).then_inc(x_in, 16)
            for c in range(RAW):
                sp.dma_start(raw[:, c, :], wts[c]).then_inc(raw_in[c], 16)
            with sp.Fori(1, 2 * G_PW1 + 1) as i:
                for r in range(RAW):
                    sp.wait_ge(lo_ready, 2 * (RAW * i + r - RAW + 1))
                    sp.dma_start(raw[:, r, :], wts[RAW * i + r]).then_inc(raw_in[r], 16)
            with sp.Fori(2 * G_PW1 + 1, 2 * G_PW2 + 1) as i:
                for r in range(RAW):
                    sp.wait_ge(raw_used, RAW * i + r - RAW + 1 - 4 * G_PW1)
                    sp.dma_start(raw[:, r, :], wts[RAW * i + r]).then_inc(raw_in[r], 16)
            with sp.Fori(2 * G_PW2 + 1, 2 * G_END) as i:
                for r in range(RAW):
                    sp.wait_ge(lo_ready, 2 * (RAW * i + r - RAW + 1) - 8 * UNSPLIT)
                    sp.dma_start(raw[:, r, :], wts[RAW * i + r]).then_inc(raw_in[r], 16)

        @block.gpsimd
        def _(pool):
            pool.wait_ge(s["mix_a"], 4)
            for n in range(3):
                src = rows[n:n + 1, :].to_broadcast([P, 8 * P])
                pool.dma_start(xg_space[:, 2 * n:2 * n + 2, :].rearrange("p a b -> p (a b)"), src).then_inc(rows_in, 16)
            pool.dma_start(xg_space[:, 6:8, :].rearrange("p a b -> p (a b)"), w_s).then_inc(rows_in, 16)
            pool.dma_start(x[:], xt).then_inc(x_again, 16)
            for j in range(4):
                pool.wait_ge(out_raw, j + 1)
                pool.dma_start(out[:, CH_K * j:CH_K * j + CH_K, :], conv[:, CH_K * j:CH_K * j + CH_K, :]).then_inc(out_done, 16)
            pool.wait_ge(out_done, 64)

        @block.scalar
        def _(act):
            def copy(dst, src):
                return nc.scalar.activation(dst, src, ACT.Copy)

            def high_part(G, i, skipped=0):
                r = i // 2 % RAW
                act.wait_ge(raw_in[r], 16 * (2 * G + i // 4 + 1))
                act.wait_ge(half_free, 8 * (G - skipped) + i + 1)
                nc.scalar.activation(whi[:, i % SPLIT].rearrange("p a b -> p (a b)"),
                                     raw[:, r, HALF * (i % 2):HALF * (i % 2) + HALF], ACT.Copy).then_inc(hi_ready, 1)

            def split(G, *ks, skipped=0):
                for k in ks:
                    if splits_on(G, k):
                        high_part(G, 11 + k, skipped)

            def copy_cross(G, par, bias=None, skipped=0):
                act.wait_ge(half_free, SPLIT + 8 * (G - skipped) + 8)
                act.wait_ge(banks_free, G + 2)
                src = ps[:, 4 * par:4 * par + 4, T:2 * T]
                if bias is None:
                    copy(cross[:], src).then_inc(cross_ready, 1)
                    return
                for t in range(CH_K):
                    ins = nc.scalar.activation(cross[:, t, :], src[:, t, :], ACT.Identity, bias=bias[:, t:t + 1])
                ins.then_inc(cross_ready, 1)

            def norm_part(e, j, xw):
                if e >= 4:
                    act.wait_ge(x_new, e - 3)
                if e:
                    act.wait_ge(ssum_part, e)
                nc.scalar.activation(padded[:, :, 0:T], xw, ACT.Square).then_inc(sq_ready, 1)
                if j is not None:
                    act.wait_ge(xg_raw, e + 1)
                    copy(xg[:, 4 * j:4 * j + 4, 0, :], total[:]).then_inc(xg_hi, 1)

            def root(n):
                act.wait_ge(ms_ready, n + 1)
                nc.scalar.activation(sq_part[:], ps[:, 7, 0:T], ACT.Sqrt, scale=1.0 / D, bias=eps).then_inc(root_ready, 1)

            eps, eps_q = param("eps"), param("eps_q")
            gate_bias = param("pw1_b")[:, KT:2 * KT]
            for i in range(4):
                high_part(0, i)
            act.wait_ge(const_in, 80)
            act.wait_ge(x_in, 16)
            copy(wba[:, :, 0, :], wba_raw[:]).then_inc(s["wba_hi"], 1)
            for j in range(4):
                norm_part(j, j, x[:, 4 * j:4 * j + 4, :])
            root(0)
            act.wait_ge(s["ba_prod"], 1)
            copy(flat_small[:, 0:32].rearrange("p (m c) -> p m c", m=TT),
                 ps[:, 6, 0:128].rearrange("p (m c) -> p m c", m=TT)[:, :, NB:2 * NB]).then_inc(s["ba_cross"], 1)
            nc.scalar.activation(flat_small[:, 128:130], ps[:, 6, 128:130], ACT.Sqrt, scale=1.0 / D, bias=eps).then_inc(s["ba_cross"], 1)
            act.wait_ge(s["ba_sum"], 1)
            nc.scalar.activation(gates[:, 0], gates[:, 5], ACT.Sigmoid).then_inc(s["beta"], 1)
            nc.scalar.activation(gates[:, 1], gates[:, 6], ACT.Abs).then_inc(act_step, 1)
            act.wait_ge(act_step, 1)
            nc.scalar.activation(gates[:, 2], gates[:, 1], ACT.Exp, scale=-1.0).then_inc(act_step, 1)
            act.wait_ge(act_step, 2)
            nc.scalar.activation(gates[:, 1], gates[:, 2], ACT.Ln, bias=1.0).then_inc(s["softplus"], 1)
            nc.scalar.activation(flat_small[:, 136:144], param("a_log"), ACT.Exp).then_inc(s["softplus"], 1)
            act.wait_ge(s["g"], 2)
            nc.scalar.activation(gates[:, 3], gates[:, 2], ACT.Exp).then_inc(s["gates"], 1)
            nc.scalar.activation(gates[:, 4], gates[:, 4], ACT.Exp).then_inc(s["gates"], 1)

            for i in range(4, 11):
                high_part(0, i)
            for G in range(G_QKVZ, G_UV):
                copy_cross(G, G % 2)
                split(G, 0, 1, 2, 3, 4, 5, 6, 7)
                act.wait_ge(s["qkvz_raw"], G + 1)
                t0 = QKVZ_AT[G]
                nc.scalar.activation(acts[:, t0:t0 + 4, :], acts[:, t0:t0 + 4, :], ACT.Silu).then_inc(s["qkvz_ready"], 1)
            for G in range(G_UV, G_WOUT):
                copy_cross(G, G % 2)
                split(G, *((0, 1, 2) if G < G_WOUT - 1 else (0,)))
                act.wait_ge(scaled, G - G_UV + 1)
                i = G - G_UV
                for a, t0 in ((0, 32 + 2 * i), (2, 40 + 2 * i)):
                    ins = nc.scalar.activation(acts[:, t0:t0 + 2, :], total[:, a:a + 2, :], ACT.Gelu)
                ins.then_inc(s["uv_ready"], 1)
                if G < G_WOUT - 1:
                    split(G, 3, 4, 5, 6, 7)

            for b in range(4):
                hh, m = b // 2, b % 2
                act.wait_ge(s["tok"], b + 1)
                if b:
                    act.wait_ge(s["mix_a"], b)
                nc.scalar.activation(buf["sq_k"], bank(0), ACT.Square)
                nc.scalar.activation(buf["sq_q"], bank(1), ACT.Square).then_inc(s["tok_sq"], 1)
                act.wait_ge(s["ss"], b + 1)
                nc.scalar.activation(sm(1, 4), sm(0, 4), ACT.Sqrt, bias=eps)
                nc.scalar.activation(sm(1, 8)[:, 4:8], sm(0, 8)[:, 4:8], ACT.Sqrt, scale=float(P), bias=eps_q).then_inc(s["root"], 1)
                act.wait_ge(s["gb"], b + 1)
                nc.scalar.activation(elast, bank(7)[:, :, C - 1::C], ACT.Exp).then_inc(s["elast"], 1)
                act.wait_ge(s["decay_in"], b + 1)
                nc.scalar.activation(buf["decay"], buf["lg"], ACT.Exp).then_inc(s["decay"], 1)
                act.wait_ge(s["feat"], b + 1)
                copy(buf["qnT"], bank(5))
                copy(buf["qdT"], bank(6)).then_inc(s["feat_act"], 1)
                act.wait_ge(s["t_prod"], b + 1)
                copy(buf["T"], bank(2)).then_inc(s["t_copy"], 1)
                for lev in range(1, LEVELS):
                    act.wait_ge(s["ut_prod"], LEVELS * b + lev)
                    copy(buf["T"], bank(5)).then_inc(s["t_copy"], 1)
                act.wait_ge(s["w_prod"], b + 1)
                nc.scalar.activation(buf["wT"], bank(6), ACT.Copy, scale=-1.0).then_inc(s["w_copy"], 1)
                for cc in range(2):
                    R = slice(C * cc, C * cc + C)
                    act.wait_ge(s["v_prod"], 2 * b + cc + 1)
                    copy(buf["v_new"][R], bank(7)[R]).then_inc(s["v_copy"], 1)
                act.wait_ge(s["s_prod"], 2 * b + 2)
                nc.scalar.activation(buf["o_sq"], bank(0), ACT.Square).then_inc(s["o_sq"], 1)
                act.wait_ge(s["o_ss"], b + 1)
                nc.scalar.activation(sm(3, 4), sm(2, 4), ACT.Sqrt, scale=1.0 / P, bias=eps).then_inc(s["o_root"], 1)
                act.wait_ge(s["gated"], b + 1)
                copy(hid[:, 4 * hh:4 * hh + 4, 0, tok(m)], buf["gate_out"]).then_inc(s["mix_hi"], 1)

            for m in range(TT):
                act.wait_ge(s["gv_center"], m + 1)
                nc.scalar.activation(wide["sq"], wide["center"], ACT.Square).then_inc(s["gv_sq"], 1)
                act.wait_ge(s["gv_ss"], m + 1)
                nc.scalar.activation(sm(6), sm(5), ACT.Sqrt, scale=1.0 / P, bias=eps).then_inc(s["gv_root"], 1)
                act.wait_ge(s["gm_out"], m + 1)
                copy(hid[:, 8:16, 0, tok(m)], wide["mixed"]).then_inc(s["gm_hi"], 1)

            split(G_WOUT - 1, 1, 2, 3, 4, 5, 6, 7)
            act.wait_ge(x_again, 16)
            for j in range(4):
                G = G_WOUT + j
                copy_cross(G, G % 2)
                split(G, 0, 1)
                norm_part(4 + j, j, x[:, 4 * j:4 * j + 4, :])
                split(G, 2, 3, 4, 5, 6, 7)

            def mlp(base, layer, q, last, last_norm):
                skipped = UNSPLIT * layer
                for j in range(4):
                    G = base + 8 * q + j
                    copy_cross(G, j % 2, skipped=skipped)
                    split(G, 0, 1, 2, skipped=skipped)
                    n = 16 * layer + 4 * q + j
                    act.wait_ge(hid_raw, n + 1)
                    copy(hid[:, 4 * j:4 * j + 4, 0, :], padded[:, :, 0:T]).then_inc(hid_hi, 1)
                    split(G, 3, 4, 5, 6, 7, skipped=skipped)
                for j in range(4):
                    G = base + 8 * q + 4 + j
                    copy_cross(G, j % 2, skipped=skipped)
                    split(G, 0, 1, skipped=skipped)
                    if last:
                        e = 8 + 8 * layer + j
                        norm_part(e, None, x[:, 4 * j:4 * j + 4, :])
                    split(G, 2, 3, 4, 5, 6, 7, skipped=skipped)

            root(1)
            with act.Fori(0, NQ - 1) as q:
                mlp(G_MLP0, 0, q, False, False)
            mlp(G_MLP0, 0, NQ - 1, True, False)

            root(2)
            with act.Fori(0, 4) as i:
                for par in range(2):
                    act.wait_ge(s["glu_scaled"], 2 * i + par + 1)
                    for t in range(2):
                        ins = nc.scalar.activation(total[:, 2 + t, :], total[:, 2 + t, :], ACT.Sigmoid,
                                                   bias=gate_bias[:, bass.ds(4 * i + 2 * par + t, 1)])
                    ins.then_inc(s["gate"], 1)
            for i in range(4):
                high_part(G_PW2, i, UNSPLIT)
            for j in range(4):
                fours = slice(4 * j, 4 * j + 4)
                act.wait_ge(s["ln_center"], j + 1)
                nc.scalar.activation(xf[:, fours, :], conv[:, fours, :], ACT.Square).then_inc(s["ln_sq"], 1)
            act.wait_ge(s["ln_ms"], 1)
            nc.scalar.activation(sq_part[:], ps[:, 6, 0:T], ACT.Sqrt, scale=1.0 / D, bias=eps).then_inc(s["ln_root"], 1)
            for j in range(4):
                act.wait_ge(s["ln_norm"], j + 1)
                for t in range(4 * j, 4 * j + 4):
                    ins = nc.scalar.activation(conv[:, t, :], conv[:, t, :], ACT.Silu, scale=param("ln_g")[:, t:t + 1],
                                               bias=param("ln_b")[:, t:t + 1])
                ins.then_inc(s["ln_act"], 1)
                act.wait_ge(s["ln_act"], j + 1)
                copy(hid[:, 4 * j:4 * j + 4, 0, :], conv[:, 4 * j:4 * j + 4, :]).then_inc(hid_hi, 1)
            for i in range(4, 11):
                high_part(G_PW2, i, UNSPLIT)
            for j in range(4):
                G = G_PW2 + j
                copy_cross(G, G % 2, bias=param("pw2_b")[:, 4 * j:4 * j + 4], skipped=UNSPLIT)
                split(G, 0, 1, skipped=UNSPLIT)
                norm_part(12 + j, j, x[:, 4 * j:4 * j + 4, :])
                split(G, 2, 3, 4, 5, 6, 7, skipped=UNSPLIT)

            root(3)
            with act.Fori(0, NQ - 1) as q:
                mlp(G_MLP1, 1, q, False, False)
            mlp(G_MLP1, 1, NQ - 1, True, True)
            root(4)

        @block.vector
        def _(dve):
            tt = nc.vector.tensor_tensor
            stt = nc.vector.scalar_tensor_tensor
            chain = [0]

            def link(ins):
                chain[0] += 1
                ins.then_inc(dve_step, 1)
                dve.wait_ge(dve_step, chain[0])

            def low_part(G, i, skipped=0):
                dve.wait_ge(hi_ready, 8 * (G - skipped) + i + 1)
                tt(wlo[:, i % SPLIT].rearrange("p a b -> p (a b)"),
                   raw[:, i // 2 % RAW, HALF * (i % 2):HALF * (i % 2) + HALF],
                   whi[:, i % SPLIT].rearrange("p a b -> p (a b)").bitcast(F32), ALU.subtract).then_inc(lo_ready, 1)

            def split(G, *ks, skipped=0):
                for k in ks:
                    if splits_on(G, k):
                        low_part(G, 11 + k, skipped)

            def leave_psum(G, par, skipped=0):
                dve.wait_ge(cross_ready, G - skipped + 1)
                tt(total[:], ps[:, 4 * par:4 * par + 4, 0:T], cross[:], ALU.add).then_inc(banks_free, 1)
                dve.wait_ge(banks_free, G + 3)

            def by_token(ap, n):
                return ap.unsqueeze(1).to_broadcast([P, n, T])

            def norm_part(e, j, gain, first, G=None, unsplit=False, skipped=0):
                xw = x[:, 4 * j:4 * j + 4, :]
                if gain is not None:
                    g = param(gain)[:, 4 * j:4 * j + 4].unsqueeze(2).to_broadcast([P, 4, T])
                    tt(xf[:, 4 * j:4 * j + 4, :] if unsplit else total[:], xw, g, ALU.mult).then_inc(xg_raw, 1)
                if G is not None:
                    split(G, 2, skipped=skipped)
                dve.wait_ge(sq_ready, e + 1)
                squares = padded[:, :, 0:T].rearrange("p n t -> p t n")
                nc.vector.tensor_reduce(ssum[:] if first else sq_part[:], squares, AX, ALU.add).then_inc(ssum_part, 1)
                dve.wait_ge(ssum_part, e + 1)
                if j == 3:
                    tt(ssum[:], ssum[:], sq_part[:], ALU.add).then_inc(ssum_ready, 1)
                    dve.wait_ge(ssum_ready, e // 4 + 1)
                elif j:
                    link(tt(ssum[:], ssum[:], sq_part[:], ALU.add))
                if G is not None:
                    split(G, 3, skipped=skipped)
                if gain is not None and not unsplit:
                    hi_parts = e + 1 - (4 if e >= 12 else 0)
                    dve.wait_ge(xg_hi, hi_parts)
                    tt(xg[:, 4 * j:4 * j + 4, 1, :], total[:], xg[:, 4 * j:4 * j + 4, 0, :].bitcast(F32),
                       ALU.subtract).then_inc(xg_ready, 1)
                    dve.wait_ge(xg_ready, hi_parts)
                if G is not None:
                    split(G, 4, 5, 6, 7, skipped=skipped)

            def rms_of(n):
                dve.wait_ge(root_ready, n + 1)
                nc.vector.reciprocal(rms[:], sq_part[:]).then_inc(rms_ready, 1)
                dve.wait_ge(rms_ready, n + 1)

            for i in range(4):
                low_part(0, i)
            dve.wait_ge(s["wba_hi"], 1)
            tt(wba[:, :, 1, :], wba_raw[:], wba[:, :, 0, :].bitcast(F32), ALU.subtract).then_inc(s["wba_ready"], 1)
            dve.wait_ge(const_in, 80)
            dve.wait_ge(x_in, 16)
            for j in range(4):
                norm_part(j, j, "e_norm", j == 0)
            rms_of(0)
            dve.wait_ge(s["ba_cross"], 2)
            ba = ps[:, 6, 0:128].rearrange("p (m c) -> p m c", m=TT)[:, :, 0:NB]
            crossed = flat_small[:, 0:32].rearrange("p (m c) -> p m c", m=TT)
            both = flat_small[:, 32:64].rearrange("p (m c) -> p m c", m=TT)
            tt(both, ba, crossed, ALU.add)
            link(nc.vector.reciprocal(flat_small[:, 130:132], flat_small[:, 128:130]))
            for m in range(TT):
                nc.vector.tensor_scalar(gates[:, 5, m], both[:, m, 0:H], flat_small[:, 130 + m:131 + m], None, ALU.mult)
                ins = nc.vector.scalar_tensor_tensor(gates[:, 6, m], both[:, m, H:2 * H], flat_small[:, 130 + m:131 + m],
                                                     param("dt_bias"), ALU.mult, ALU.add)
            ins.then_inc(s["ba_sum"], 1)
            dve.wait_ge(s["softplus"], 2)
            link(stt(gates[:, 1], gates[:, 6], 0.0, gates[:, 1], ALU.max, ALU.add))
            stt(gates[:, 1], gates[:, 1], -1.0, flat_small[:, 136:144].unsqueeze(1).to_broadcast([P, TT, H]),
                ALU.mult, ALU.mult).then_inc(s["g"], 1)
            dve.wait_ge(s["gc_prod"], 1)
            link(nc.vector.tensor_copy(gates[:, 2], ps[:, 6, 0:16].rearrange("p (m h) -> p m h", m=TT)))
            tt(gates[:, 4], ps[:, 6, 16:32].rearrange("p (m h) -> p m h", m=TT), gates[:, 2], ALU.subtract).then_inc(s["g"], 1)

            link(nc.vector.memset(padded[:, :, 0:3], 0.0))
            for i in range(4, 11):
                low_part(0, i)
            for G in range(G_QKVZ, G_UV):
                leave_psum(G, G % 2)
                split(G, 0)
                t0 = QKVZ_AT[G]
                if G >= 6:
                    tt(acts[:, t0:t0 + 4, :], total[:], by_token(rms[:], 4), ALU.mult).then_inc(s["qkvz_raw"], 1)
                    split(G, 1, 2, 3, 4, 5, 6, 7)
                    continue
                link(tt(padded[:, :, 3:3 + T], total[:], by_token(rms[:], 4), ALU.mult))
                for k in range(4):
                    for t in range(4):
                        w = cw[:, t0 + t, k:k + 1]
                        dst, src = acts[:, t0 + t, :], padded[:, t, k:k + T]
                        if k == 0:
                            ins = nc.vector.tensor_scalar(dst, src, w, None, ALU.mult)
                        else:
                            ins = stt(dst, src, w, dst, ALU.mult, ALU.add)
                    if k < 3:
                        link(ins)
                        split(G, k + 1)
                ins.then_inc(s["qkvz_raw"], 1)
                split(G, 4, 5, 6, 7)
            for G in range(G_UV, G_WOUT):
                if G > G_UV:
                    dve.wait_ge(s["uv_ready"], G - G_UV)
                leave_psum(G, G % 2)
                split(G, 0)
                tt(total[:], total[:], by_token(rms[:], 4), ALU.mult).then_inc(scaled, 1)
                if G < G_WOUT - 1:
                    split(G, 1, 2, 3, 4, 5, 6, 7)

            for b in range(4):
                hh, m = b // 2, b % 2
                heads = slice(HH * hh, HH * hh + HH)
                beta, g, gc, eg, et = (gates[:, i, m, heads] for i in range(5))
                if b == 0:
                    dve.wait_ge(half_free, SPLIT + 8 * G_WOUT)
                    dve.wait_ge(s["gates"], 2)
                tt(buf["lg"], all_heads(const("upto")), per_head(g), ALU.mult).then_inc(s["lg"], 1)
                dve.wait_ge(s["tok_sq"], b + 1)
                nc.vector.tensor_reduce(sm(0, 4), buf["sq_k"], AX, ALU.add)
                nc.vector.tensor_reduce(sm(0, 8)[:, 4:8], buf["sq_q"], AX, ALU.add).then_inc(s["ss"], 1)
                dve.wait_ge(s["root"], b + 1)
                link(nc.vector.reciprocal(sm(4), sm(1)))
                tt(buf["kn"], bank(0), per_head(sm(4, 4)), ALU.mult)
                tt(buf["qn"], bank(1), per_head(sm(4, 8)[:, 4:8]), ALU.mult)
                link(tt(buf["vb"], bank(2), per_head(beta), ALU.mult))
                tt(buf["kt"], buf["kn"], per_head(et), ALU.mult)
                tt(buf["qd"], buf["qn"], per_head(eg), ALU.mult)
                tt(buf["kb"], buf["kn"], per_head(beta), ALU.mult).then_inc(s["normed"], 1)
                dve.wait_ge(s["elast"], b + 1)
                link(tt(buf["lg"], bank(7), per_head(gc), ALU.subtract))
                tt(buf["lg"], buf["lg"], all_heads(const("fill")), ALU.min).then_inc(s["decay_in"], 1)
                tt(buf["kd"], buf["kb"], per_head(eg), ALU.mult)
                dve.wait_ge(s["feat"], b + 1)
                nc.vector.tensor_copy(buf["knT"], bank(3))
                nc.vector.tensor_copy(buf["kbT"], bank(4)).then_inc(s["feat_dve"], 1)
                dve.wait_ge(s["decay"], b + 1)
                link(tt(buf["decay_s"], buf["decay"], all_heads(const("strict")), ALU.mult))
                dve.wait_ge(s["prods"], b + 1)
                tt(buf["attnT"], bank(1), buf["decay"], ALU.mult)
                link(tt(buf["C"], bank(0), buf["decay_s"], ALU.mult))
                link(tt(buf["C"], buf["C"], all_heads(const("ident")), ALU.add))
                tt(buf["U"], buf["C"], all_heads(const("lev0t")), ALU.mult).then_inc(s["inv0"], 1)
                for lev in range(1, LEVELS + 1):
                    dve.wait_ge(s["y_prod"], LEVELS * b + lev)
                    tt(buf["Z"], bank(3), all_heads(const(f"lev{lev}")), ALU.mult).then_inc(s["z"], 1)
                    dve.wait_ge(s["ut_prod"], LEVELS * b + lev)
                    nc.vector.tensor_copy(buf["U"], bank(4)).then_inc(s["u_copy"], 1)
                if m == 0:
                    nc.vector.memset(buf["state"], 0.0).then_inc(s["state"], 1)
                for cc in range(2):
                    if m == 0 or cc == 1:
                        dve.wait_ge(s["state"], 5 * hh + 2 * m + cc + 1)
                    link(tt(buf["state_d"], buf["state"], elast[:, :, cc].unsqueeze(2).to_broadcast([P, HH, P]), ALU.mult))
                    dve.wait_ge(s["s_prod"], 2 * b + cc + 1)
                    tt(buf["state"], bank(1), buf["state_d"], ALU.add).then_inc(s["state"], 1)
                dve.wait_ge(s["o_sq"], b + 1)
                nc.vector.tensor_reduce(sm(2, 4), buf["o_sq"], AX, ALU.add).then_inc(s["o_ss"], 1)
                dve.wait_ge(s["o_root"], b + 1)
                link(nc.vector.reciprocal(sm(7, 4), sm(3, 4)))
                tt(buf["o_n"], bank(0), per_head(sm(7, 4)), ALU.mult).then_inc(s["o_norm"], 1)
                dve.wait_ge(s["o_prod"], b + 1)
                z0 = 24 + HH * hh
                stt(buf["gate_out"], bank(2), param("head_norm"), acts[:, z0:z0 + HH, tok(m)], ALU.mult,
                    ALU.mult).then_inc(s["gated"], 1)
                dve.wait_ge(s["mix_hi"], b + 1)
                dst = hid[:, HH * hh:HH * hh + HH, :, tok(m)]
                tt(dst[:, :, 1, :], buf["gate_out"], dst[:, :, 0, :].bitcast(F32), ALU.subtract).then_inc(s["mix_a"], 1)

            for m in range(TT):
                if m == 0:
                    dve.wait_ge(rows_in, 64)
                    nc.vector.memset(wide["w_s"][C:P, :, 0:C], 0.0)
                dve.wait_ge(s["gv_prod"], m + 1)
                wide_of = lambda ap: ap.unsqueeze(2).to_broadcast([P, 8, P])
                link(nc.vector.tensor_reduce(sm(8), pair(0), AX, ALU.add))
                link(nc.vector.tensor_scalar(sm(8), sm(8), 1.0 / P, None, ALU.mult))
                tt(wide["center"], pair(0), wide_of(sm(8)), ALU.subtract).then_inc(s["gv_center"], 1)
                dve.wait_ge(s["gv_sq"], m + 1)
                nc.vector.tensor_reduce(sm(5), wide["sq"], AX, ALU.add).then_inc(s["gv_ss"], 1)
                dve.wait_ge(s["gv_root"], m + 1)
                link(nc.vector.reciprocal(sm(4), sm(6)))
                link(tt(wide["center"], wide["center"], wide_of(sm(4)), ALU.mult))
                link(tt(wide["center"], wide["center"], wide["ln_g"], ALU.mult))
                tt(wide["center"], wide["center"], wide["ln_b"], ALU.add).then_inc(s["gv_norm"], 1)
                dve.wait_ge(s["mixed"], m + 1)
                link(tt(wide["mixed"], pair(2), wide["b_s"], ALU.add))
                tt(wide["mixed"], wide["mixed"], acts[:, 32:40, tok(m)], ALU.mult).then_inc(s["gm_out"], 1)
                dve.wait_ge(s["gm_hi"], m + 1)
                dst = hid[:, 8:16, :, tok(m)]
                tt(dst[:, :, 1, :], wide["mixed"], dst[:, :, 0, :].bitcast(F32), ALU.subtract).then_inc(s["mix_b"], 1)

            split(G_WOUT - 1, 1, 2, 3, 4, 5, 6, 7)
            dve.wait_ge(x_again, 16)

            def onto_residual(G, par, j, e, gain, part=0, skipped=0):
                leave_psum(G, par, skipped)
                split(G, 0, skipped=skipped)
                ins = tt(x[:, 4 * j:4 * j + 4, :], x[:, 4 * j:4 * j + 4, :], total[:], ALU.add)
                if e is not None:
                    ins.then_inc(x_new, 1)
                    dve.wait_ge(x_new, e - 3)
                    split(G, 1, skipped=skipped)
                    norm_part(e, j, gain, j == 0, G, gain == "o_norm", skipped)
                else:
                    ins.then_inc(x_part, 1)
                    dve.wait_ge(x_part, part + 1)
                    split(G, 1, 2, 3, 4, 5, 6, 7, skipped=skipped)

            for j in range(4):
                onto_residual(G_WOUT + j, j % 2, j, 4 + j, "f_norm0")

            def mlp(base, layer, q, last, gain):
                skipped = UNSPLIT * layer
                for j in range(4):
                    G = base + 8 * q + j
                    n = 16 * layer + 4 * q + j
                    leave_psum(G, j % 2, skipped)
                    split(G, 0, skipped=skipped)
                    tt(total[:], total[:], by_token(rms[:], 4), ALU.mult).then_inc(hid_scaled, 1)
                    split(G, 1, skipped=skipped)
                    dve.wait_ge(hid_scaled, n + 1)
                    stt(padded[:, :, 0:T], total[:], 0.0, total[:], ALU.max, ALU.mult).then_inc(hid_raw, 1)
                    split(G, 2, skipped=skipped)
                    dve.wait_ge(hid_hi, n + 4 * layer + 1)
                    tt(hid[:, 4 * j:4 * j + 4, 1, :], padded[:, :, 0:T], hid[:, 4 * j:4 * j + 4, 0, :].bitcast(F32),
                       ALU.subtract).then_inc(hid_ready, 1)
                    dve.wait_ge(hid_ready, n + 4 * layer + 1)
                    split(G, 3, 4, 5, 6, 7, skipped=skipped)
                for j in range(4):
                    G = base + 8 * q + 4 + j
                    onto_residual(G, j % 2, j, 8 + 8 * layer + j if last else None, gain, 12 * layer + 4 * q + j,
                                  skipped)

            rms_of(1)
            with dve.Fori(0, NQ - 1) as q:
                mlp(G_MLP0, 0, q, False, None)
            mlp(G_MLP0, 0, NQ - 1, True, "o_norm")

            rms_of(2)
            nc.vector.memset(ssum[:], 0.0)
            link(nc.vector.memset(zwin[:, :, 0:32], 0.0))
            with dve.Fori(0, 4) as i:
                for par in range(2):
                    n = 2 * i + par
                    dve.wait_ge(raw_used, 4 * n + 4)
                    tt(total[:], ps[:, 4 * par:4 * par + 4, 0:T], by_token(rms[:], 4), ALU.mult).then_inc(s["glu_scaled"], 1)
                    dve.wait_ge(s["gate"], n + 1)
                    tile0 = 4 * i + 2 * par
                    z = [zwin[:, 2 * par + t, :] for t in range(2)]
                    acc = [conv[:, bass.ds(tile0 + t, 1), :].rearrange("p a t -> p (a t)") for t in range(2)]
                    for t in range(2):
                        ins = stt(z[t][:, 32:32 + T], total[:, t, :], param("pw1_b")[:, bass.ds(tile0 + t, 1)],
                                  total[:, 2 + t, :], ALU.add, ALU.mult)
                    ins.then_inc(banks_free, 1)
                    dve.wait_ge(banks_free, G_PW1 + n + 3)
                    for k in range(WD):
                        for t in range(2):
                            src = z[t][:, 2 + k:2 + k + T]
                            w = dwt[:, bass.ds(tile0 + t, 1), k:k + 1].rearrange("p a t -> p (a t)")
                            if k == 0:
                                ins = nc.vector.tensor_scalar(acc[t], src, w, param("dw_b")[:, bass.ds(tile0 + t, 1)],
                                                              ALU.mult, ALU.add)
                            else:
                                dve.wait_ge(s["taps0" if t == 0 else "taps1"], WD * n + k)
                                ins = stt(acc[t], src, w, acc[t], ALU.mult, ALU.add)
                            ins.then_inc(s["taps0" if t == 0 else "taps1"], 1)
                    for t in range(2):
                        dve.wait_ge(s["taps0" if t == 0 else "taps1"], WD * n + WD)
                        tt(ssum[:], ssum[:], acc[t], ALU.add).then_inc(s["ln_sum"], 1)
                        dve.wait_ge(s["ln_sum"], 2 * n + t + 1)
            for i in range(4):
                low_part(G_PW2, i, UNSPLIT)
            dve.wait_ge(s["ln_mean"], 1)
            link(nc.vector.tensor_scalar(rms[:], ps[:, 7, 0:T], 1.0 / D, None, ALU.mult))
            for j in range(4):
                w = conv[:, 4 * j:4 * j + 4, :]
                tt(w, w, by_token(rms[:], 4), ALU.subtract).then_inc(s["ln_center"], 1)
            dve.wait_ge(s["ln_center"], 4)
            dve.wait_ge(s["ln_root"], 1)
            link(nc.vector.reciprocal(rms[:], sq_part[:]))
            for j in range(4):
                w = conv[:, 4 * j:4 * j + 4, :]
                tt(w, w, by_token(rms[:], 4), ALU.mult).then_inc(s["ln_norm"], 1)
            for j in range(4):
                dve.wait_ge(hid_hi, 17 + j)
                tt(hid[:, 4 * j:4 * j + 4, 1, :], conv[:, 4 * j:4 * j + 4, :], hid[:, 4 * j:4 * j + 4, 0, :].bitcast(F32),
                   ALU.subtract).then_inc(hid_ready, 1)
            for i in range(4, 11):
                low_part(G_PW2, i, UNSPLIT)
            for j in range(4):
                onto_residual(G_PW2 + j, j % 2, j, 12 + j, "f_norm1", skipped=UNSPLIT)

            rms_of(3)
            with dve.Fori(0, NQ - 1) as q:
                mlp(G_MLP1, 1, q, False, None)
            mlp(G_MLP1, 1, NQ - 1, True, None)
            rms_of(4)
            for j in range(4):
                w = conv[:, 4 * j:4 * j + 4, :]
                g = param("final_norm")[:, 4 * j:4 * j + 4].unsqueeze(2).to_broadcast([P, 4, T])
                link(tt(w, x[:, 4 * j:4 * j + 4, :], by_token(rms[:], 4), ALU.mult))
                tt(w, w, g, ALU.mult).then_inc(out_raw, 1)

        @block.tensor
        def _(pe):
            mm = nc.tensor.matmul

            def group(G, par, operand, ready, counts, skipped=0, norm=None):
                pe.wait_ge(banks_free, G + 1)
                for i in range(8):
                    if norm is not None and i == 6:
                        mean_squares(norm, G)
                    pe.wait_ge(lo_ready, 8 * (G - skipped) + i + 1)
                    if ready is not None and i % 2 == 0:
                        pe.wait_ge(ready, counts + i // 2)
                    r = i % SPLIT
                    for k in range(CH_K // 2):
                        kt = CH_K // 2 * i + k
                        for n in range(4):
                            cols = slice(P * n, P * n + P)
                            mm(ps[:, 4 * par + n, :], whi[:, r, k, cols], operand[:, kt].rearrange("p a t -> p (a t)"),
                               start=(kt == 0), stop=False)
                            ins = mm(ps[:, 4 * par + n, T:2 * T], wlo[:, r, k, cols], operand[:, kt, 0, :],
                                     start=False, stop=(kt == KT - 1))
                    ins.then_inc(half_free, 1)

            def unsplit_group(G, par, norm=None):
                pe.wait_ge(banks_free, G + 1)
                for kc in range(4):
                    if norm is not None and kc == 3:
                        mean_squares(norm, G)
                    r = kc % RAW
                    pe.wait_ge(raw_in[r], 16 * (2 * G + kc // 2 + 1))
                    if norm is not None:
                        pe.wait_ge(xg_raw, 4 * norm + kc + 1)
                    for k in range(CH_K):
                        kt = CH_K * kc + k
                        for n in range(4):
                            ins = mm(ps[:, 4 * par + n, 0:T], raw[:, r, CH_N * k + P * n:CH_N * k + P * n + P],
                                     xf[:, kt, :], start=(kt == 0), stop=(kt == KT - 1))
                    ins.then_inc(raw_used, 1)

            def mean_squares(n, G=None):
                pe.wait_ge(ssum_ready, n + 1)
                if G is not None:
                    pe.wait_ge(banks_free, G + 2)
                mm(ps[:, 7, 0:T], const("ones"), ssum[:], start=True, stop=True).then_inc(ms_ready, 1)

            pe.sem_inc(half_free, SPLIT)
            pe.sem_inc(banks_free, 2)
            mean_squares(0)
            pe.wait_ge(s["wba_ready"], 1)
            pe.wait_ge(xg_ready, 4)
            for m in range(TT):
                for kt in range(KT):
                    mm(ps[:, 6, 64 * m:64 * m + 2 * NB], xg[:, kt, 0, tok(m)], wba[:, kt].rearrange("p a b -> p (a b)"),
                       start=(kt == 0), stop=False)
                    mm(ps[:, 6, 64 * m + NB:64 * m + 2 * NB], xg[:, kt, 1, tok(m)], wba[:, kt, 0, :],
                       start=False, stop=(kt == KT - 1))
            for m in range(TT):
                ins = mm(ps[:, 6, 128 + m:129 + m], ssum[:, tok(m)], const("ones")[:, 0:1], start=True, stop=True)
            ins.then_inc(s["ba_prod"], 1)
            pe.wait_ge(s["g"], 1)
            mm(ps[:, 6, 0:16], const("upto"), gates[:, 1].rearrange("p m h -> p (m h)"), start=True, stop=True)
            mm(ps[:, 6, 16:32], const("chunk"), gates[:, 1].rearrange("p m h -> p (m h)"), start=True,
               stop=True).then_inc(s["gc_prod"], 1)
            pe.wait_ge(s["gates"], 2)
            pe.wait_ge(root_ready, 1)
            with pe.Fori(0, G_WOUT // 2) as i:
                for par in range(2):
                    group(2 * i + par, par, xg, None, 0)

            def transposes(b, src):
                for h in range(HH):
                    ins = nc.tensor.transpose(bank(b)[:, h, :], src(h), const("ident"))
                return ins

            def products(b, left, right):
                for h in range(HH):
                    ins = mm(bank(b)[:, h, :], left[:, h, :], right[:, h, :], start=True, stop=True)
                return ins

            pe.wait_ge(banks_free, 2 + G_WOUT)
            pe.wait_ge(s["qkvz_ready"], 8)
            for b in range(4):
                hh, m = b // 2, b % 2
                if b:
                    pe.wait_ge(s["gated"], b)
                transposes(0, lambda h: acts[:, 8 + HH * hh + h, tok(m)])
                transposes(1, lambda h: acts[:, HH * hh + h, tok(m)])
                transposes(2, lambda h: acts[:, 16 + HH * hh + h, tok(m)]).then_inc(s["tok"], 1)
                pe.wait_ge(s["lg"], b + 1)
                mm(ps[:, 7, :], const("ones"), buf["lg"].rearrange("p h c -> p (h c)"), start=True, stop=True).then_inc(s["gb"], 1)
                pe.wait_ge(s["normed"], b + 1)
                transposes(3, lambda h: buf["kn"][:, h, :])
                transposes(4, lambda h: buf["kb"][:, h, :])
                transposes(5, lambda h: buf["qn"][:, h, :])
                transposes(6, lambda h: buf["qd"][:, h, :]).then_inc(s["feat"], 1)
                pe.wait_ge(s["feat_dve"], b + 1)
                pe.wait_ge(s["feat_act"], b + 1)
                products(0, buf["knT"], buf["kbT"])
                products(1, buf["knT"], buf["qnT"]).then_inc(s["prods"], 1)
                pe.wait_ge(s["inv0"], b + 1)
                transposes(2, lambda h: buf["U"][:, h, :]).then_inc(s["t_prod"], 1)
                for lev in range(1, LEVELS + 1):
                    pe.wait_ge(s["t_copy"], LEVELS * b + lev)
                    if lev > 1:
                        pe.wait_ge(s["u_copy"], LEVELS * b + lev - 1)
                    products(3, buf["C"], buf["T"]).then_inc(s["y_prod"], 1)
                    pe.wait_ge(s["z"], LEVELS * b + lev)
                    ins = products(4, buf["Z"], buf["U"])
                    if lev < LEVELS:
                        ins = products(5, buf["U"], buf["Z"])
                    ins.then_inc(s["ut_prod"], 1)
                pe.wait_ge(s["u_copy"], LEVELS * b + LEVELS)
                products(6, buf["kd"], buf["U"]).then_inc(s["w_prod"], 1)
                pe.wait_ge(s["w_copy"], b + 1)
                for cc in range(2):
                    R = slice(C * cc, C * cc + C)
                    pe.wait_ge(s["state"], 5 * hh + 2 * m + cc + 1)
                    for h in range(HH):
                        mm(bank(7)[R, h, :], buf["U"][:, h, R], buf["vb"][:, h, :], start=True, stop=False)
                        ins = mm(bank(7)[R, h, :], buf["wT"][:, h, R], buf["state"][:, h, :], start=False, stop=True)
                    ins.then_inc(s["v_prod"], 1)
                    pe.wait_ge(s["v_copy"], 2 * b + cc + 1)
                    for h in range(HH):
                        mm(bank(0)[R, h, :], buf["qdT"][:, h, R], buf["state"][:, h, :], start=True, stop=False)
                        mm(bank(0)[R, h, :], buf["attnT"][R, h, R], buf["v_new"][R, h, :], start=False, stop=True)
                    for h in range(HH):
                        ins = mm(bank(1)[:, h, :], buf["kt"][R, h, :], buf["v_new"][R, h, :], start=True, stop=True)
                    ins.then_inc(s["s_prod"], 1)
                pe.wait_ge(s["o_norm"], b + 1)
                transposes(2, lambda h: buf["o_n"][:, h, :]).then_inc(s["o_prod"], 1)

            for m in range(TT):
                if m == 0:
                    pe.wait_ge(s["mix_a"], 4)
                    pe.wait_ge(s["uv_ready"], 4)
                else:
                    pe.wait_ge(s["gv_center"], m)
                for g in range(8):
                    ins = nc.tensor.transpose(pair(0)[:, g, :], acts[:, 40 + g, tok(m)], const("ident"))
                ins.then_inc(s["gv_prod"], 1)
                pe.wait_ge(s["gv_norm"], m + 1)
                for g in range(8):
                    ins = mm(pair(2)[:, g, :], wide["center"][:, g, :], wide["w_s"][:, g, :], start=True, stop=True)
                ins.then_inc(s["mixed"], 1)

            pe.wait_ge(s["mix_b"], 2)
            with pe.Fori(0, 2) as i:
                for par in range(2):
                    group(G_WOUT + 2 * i + par, par, hid, None, 0)

            def mlp(base, layer):
                skipped, fours = UNSPLIT * layer, 4 * layer
                xg_count, norm = 5 + 4 * layer, 1 + 2 * layer
                for j in range(4):
                    group(base + j, j % 2, xg, xg_ready, xg_count, skipped, norm if j == 0 else None)
                    if j == 0:
                        pe.wait_ge(root_ready, norm + 1)
                with pe.Fori(0, 2) as i:
                    for par in range(2):
                        group(base + 4 + 2 * i + par, par, hid, hid_ready, 20 * layer + 1, skipped)
                with pe.Fori(1, NQ) as q:
                    with pe.Fori(0, 2) as i:
                        for par in range(2):
                            group(base + 8 * q + 2 * i + par, par, xg, None, 0, skipped)
                    with pe.Fori(0, 2) as i:
                        for par in range(2):
                            group(base + 8 * q + 4 + 2 * i + par, par, hid, hid_ready, 20 * layer + 4 * q + 1, skipped)

            mlp(G_MLP0, 0)
            unsplit_group(G_PW1, 0, norm=2)
            pe.wait_ge(root_ready, 3)
            unsplit_group(G_PW1 + 1, 1)
            with pe.Fori(1, 4) as i:
                for par in range(2):
                    unsplit_group(G_PW1 + 2 * i + par, par)
            pe.wait_ge(s["ln_sum"], KT)
            mm(ps[:, 7, 0:T], const("ones"), ssum[:], start=True, stop=True).then_inc(s["ln_mean"], 1)
            for kt in range(KT):
                pe.wait_ge(s["ln_sq"], kt // 4 + 1)
                ins = mm(ps[:, 6, 0:T], const("ones"), xf[:, kt, :], start=(kt == 0), stop=(kt == KT - 1))
            ins.then_inc(s["ln_ms"], 1)
            pe.wait_ge(s["ln_root"], 1)
            with pe.Fori(0, 2) as i:
                for par in range(2):
                    group(G_PW2 + 2 * i + par, par, hid, hid_ready, 17, UNSPLIT)
            mlp(G_MLP1, 1)
            mean_squares(4)


_INS = ["xt", "wts", "w_ba", "consts", "params", "conv_w", "dw", "rows", "w_s"]


def tables():
    import numpy as np
    i = np.arange(P)
    same = i[:, None] // C == i[None, :] // C
    upto = same & (i[:, None] <= i[None, :])
    t = {"ident": np.eye(P), "ones": np.ones((P, P)), "upto": upto, "chunk": same,
         "fill": np.where(upto, 3e38, -3e38), "strict": upto & (i[:, None] < i[None, :])}
    for lev in range(LEVELS + 1):
        size = 1 << lev
        below = (i[:, None] // (2 * size) == i[None, :] // (2 * size)) & (i[:, None] // size > i[None, :] // size)
        m = np.eye(P) - below
        t["lev0t" if lev == 0 else f"lev{lev}"] = m.T if lev == 0 else m
    return np.ascontiguousarray(np.stack([t[n] for n in CONSTS], 1).astype(np.float32))


def kernel(**inputs):
    import numpy as np
    import concourse.bacc as bacc
    from concourse.bass_utils import run_bass_kernel_spmd as run

    a = {n: np.asarray(v) for n, v in inputs.items()}

    def chunks(w):
        w = w.reshape(4, CH_K, P, -1, CH_N)
        return w.transpose(3, 0, 2, 1, 4).reshape(-1, P, CH)

    def tiles(v):
        return v.reshape(-1, P).T

    w_in = a["e_w_in"][0]
    hd = H * P
    q, k, v, z = (w_in[:, i * hd:(i + 1) * hd] for i in range(4))
    ba = w_in[:, 4 * hd:4 * hd + NB]
    u, vr = (w_in[:, 4 * hd + NB + i * hd:4 * hd + NB + (i + 1) * hd] for i in range(2))
    half = CH_N
    cols = [q[:, :half], k[:, :half], v[:, :half], q[:, half:], k[:, half:], v[:, half:], z]
    for i in range(4):
        cols += [u[:, 256 * i:256 * i + 256], vr[:, 256 * i:256 * i + 256]]
    parts = [chunks(np.concatenate(cols, 1)), chunks(a["e_w_out"][0])]

    def mlp(layer):
        for i in range(NQ):
            parts.append(chunks(a["f_w1"][layer][:, i * D:(i + 1) * D]))
            parts.append(chunks(a["f_w2"][layer][i * D:(i + 1) * D]))

    mlp(0)
    pw1 = a["o_pw1"][0]
    cols = []
    for i in range(8):
        cols += [pw1[:, 256 * i:256 * i + 256], pw1[:, D + 256 * i:D + 256 * i + 256]]
    parts += [chunks(np.concatenate(cols, 1)), chunks(a["o_pw2"][0])]
    mlp(1)
    wide = lambda v: np.broadcast_to(v[None, :], (P, v.size))
    params = {"e_norm": tiles(a["e_norm"][0]), "f_norm0": tiles(a["f_norm"][0]), "o_norm": tiles(a["o_norm"][0]),
              "f_norm1": tiles(a["f_norm"][1]), "final_norm": tiles(a["final_norm"]), "pw1_b": tiles(a["o_pw1_b"][0]),
              "dw_b": tiles(a["o_dw_b"][0]), "ln_g": tiles(a["o_ln_g"][0]), "ln_b": tiles(a["o_ln_b"][0]),
              "pw2_b": tiles(a["o_pw2_b"][0]), "head_norm": tiles(a["e_o_norm"][0]), "a_log": wide(a["e_a_log"][0]),
              "dt_bias": wide(a["e_dt_bias"][0]), "eps": np.full((P, 1), EPS, np.float32),
              "eps_q": np.full((P, 1), EPS * P, np.float32)}
    arrays = {
        "xt": a["x"][0].T.reshape(KT, P, T).transpose(1, 0, 2),
        "wts": np.concatenate(parts, 0),
        "w_ba": ba.reshape(KT, P, NB).transpose(1, 0, 2),
        "consts": tables(),
        "params": np.concatenate([params[n] for n in PARAMS], 1),
        "conv_w": a["e_conv_w"][0].reshape(4, 24, P).transpose(2, 1, 0),
        "dw": a["o_dw"][0].reshape(WD, KT, P).transpose(2, 1, 0),
        "rows": np.stack([a["e_ln_g"][0], a["e_ln_b"][0], a["e_b_s"][0].reshape(-1)]),
        "w_s": a["e_w_s"][0].transpose(2, 0, 1).reshape(P, 8 * P),
    }
    arrays = {n: np.ascontiguousarray(v) for n, v in arrays.items()}
    nc = bacc.Bacc("TRN2", target_bir_lowering=False, num_devices=1)
    args = [nc.dram_tensor(f"in_{n}", arrays[n].shape, F32, kind="ExternalInput").ap() for n in _INS]
    out = nc.dram_tensor("out_t", (P, KT, T), F32, kind="ExternalOutput").ap()
    build(nc, *args, out)
    r = run(nc, [{f"in_{n}": v for n, v in arrays.items()}], core_ids=[0])
    return r.results[0]["out_t"].transpose(1, 0, 2).reshape(1, D, T).transpose(0, 2, 1)
```

```python
from contextlib import ExitStack

import concourse.bass as bass
from concourse import mybir
from concourse.alu_op_type import AluOpType as ALU

F32 = mybir.dt.float32
F32R = mybir.dt.float32r
ACT = mybir.ActivationFunctionType
AX = mybir.AxisListType.X

P = 128
D = 2048
T = 256
KT = D // P
TT = T // P
H = 8
HH = 4
C = 64
NQ = 4
NB = 16
WD = 31
CH_K = 4
CH_N = 512
CH = CH_K * CH_N
RAW = 2
HALF = CH // 2
SPLIT = 4
G_QKVZ, G_UV, G_WOUT, G_MLP0, G_PW1, G_PW2, G_MLP1, G_END = 0, 8, 12, 16, 48, 56, 60, 92
NEVER = 1 << 30
GATES_START, BLOCK_START, BLOCK_TIME = 32, 59, 33
AT = {"tok": 0, "gb": 8, "feat": 10, "attn": 12, "t_prod": 14, "levels": 15, "w": 25, "chunks": 26, "o": 31}
UV_ROWS, UV_MIX = 6, 12
NARROW_BANK = [0, 2] * 6 + [0, 4, 6, 4]
UNSPLIT = G_PW2 - G_PW1
WARM = 12
EPS = 1e-6
QKVZ_AT = [0, 8, 16, 24, 4, 12, 20, 28]
LEVELS = 5

CONSTS = ["ident", "ones", "upto", "chunk", "fill", "strict", "lev0t"] + [f"lev{i}" for i in range(1, LEVELS + 1)]
PARAMS, _at = {}, 0
for _n, _w in (("e_norm", KT), ("f_norm0", KT), ("o_norm", KT), ("f_norm1", KT), ("final_norm", KT),
               ("pw1_b", 2 * KT), ("dw_b", KT), ("ln_g", KT), ("ln_b", KT), ("pw2_b", KT),
               ("head_norm", 1), ("a_log", H), ("dt_bias", H), ("eps", 1), ("eps_q", 1)):
    PARAMS[_n] = (_at, _at + _w)
    _at += _w
N_PARAMS = _at


def splits_on(G, k):
    if not isinstance(G, int):
        return True
    half = 8 * G + 11 + k
    return half < 8 * G_PW1 or 8 * G_PW2 <= half < 8 * G_END and G >= G_PW2


def build(nc, xt, wts, w_ba, consts, params, conv_w, dw, rows, w_s, out):
    with ExitStack() as ctx:
        def sb(name, shape, dt=F32):
            return ctx.enter_context(nc.sbuf_tensor(name, shape, dt))

        def sem(name):
            return ctx.enter_context(nc.semaphore(name))

        used = (nc.sbuf_base + 63) // 64 * 64
        sb("arena", [P, 8192 + 4096 + 32])
        xg = nc.alloc_sbuf_tensor_at("xg", [P, KT, 2, T], F32R, offset=used)
        x = nc.alloc_sbuf_tensor_at("x", [P, KT, T], F32, offset=used + 32768)
        x_space = nc.alloc_sbuf_tensor_at("x_space", [P, 8, 512], F32, offset=used + 32768)
        hid = sb("hid", [P, KT, 2, T], F32R)
        raw = sb("raw", [P, RAW, CH])
        whi = sb("whi", [P, SPLIT, CH_K // 2, CH_N], F32R)
        wlo = sb("wlo", [P, SPLIT, CH_K // 2, CH_N], F32R)
        work = sb("work", [P, 12288])
        cross = sb("cross", [P, CH_K, T])
        total = sb("total", [P, CH_K, T])
        padded = sb("padded", [P, CH_K, T + 4])
        ct = sb("ct", [P, len(CONSTS), P])
        pt = sb("pt", [P, N_PARAMS])
        cw = sb("cw", [P, 24, 4])
        dwt = sb("dwt", [P, KT, WD])
        rms = sb("rms", [P, T])
        ssum = sb("ssum", [P, T])
        sq_part = sb("sq_part", [P, T])
        wba_raw = sb("wba_raw", [P, KT, NB])
        wba = sb("wba", [P, KT, 2, NB], F32R)
        gates = sb("gates", [P, 8, TT, H])
        small = sb("small", [P, 16, TT, H])
        ps = ctx.enter_context(nc.psum_tensor("ps", [P, 8, 512], F32))

        def const(name):
            return ct[:, CONSTS.index(name), :]

        def param(name):
            a, b = PARAMS[name]
            return pt[:, a:b]

        acts = work[:].rearrange("p (n t) -> p n t", t=T)
        conv = work[:, 0:KT * T].rearrange("p (n t) -> p n t", t=T)
        xf = work[:, KT * T:2 * KT * T].rearrange("p (n t) -> p n t", t=T)
        zwin = work[:, 2 * KT * T:2 * KT * T + 4 * (T + 32)].rearrange("p (n t) -> p n t", t=T + 32)

        def bank(b):
            return ps[:, b, :].rearrange("p (h c) -> p h c", h=HH)

        def per_head(ap):
            return ap.unsqueeze(2).to_broadcast([P, HH, P])

        def all_heads(ap):
            return ap.unsqueeze(1).to_broadcast([P, HH, P])

        pivot = cross[:, 0, :]

        raw_in = [sem(f"raw_in{i}") for i in range(RAW)]
        table_in, dw_in = sem("table_in"), sem("dw_in")
        const_in, rows_in, x_again = sem("const_in"), sem("rows_in"), sem("x_again")
        x_in = [sem(f"x_in{j}") for j in range(4)]
        hi_ready, lo_ready = sem("hi_ready"), sem("lo_ready")
        raw_used = sem("raw_used")
        half_free = sem("half_free")
        cross_ready = sem("cross_ready")
        banks_free = sem("banks_free")
        hid_scaled = sem("hid_scaled")
        xg_raw, xg_hi, xg_ready = sem("xg_raw"), sem("xg_hi"), sem("xg_ready")
        hid_raw, hid_hi, hid_ready = sem("hid_raw"), sem("hid_hi"), sem("hid_ready")
        x_part = sem("x_part")
        x_new = sem("x_new")
        sq_ready, ssum_part, ssum_ready = sem("sq_ready"), sem("ssum_part"), sem("ssum_ready")
        ms_ready, root_ready, rms_ready = sem("ms_ready"), sem("root_ready"), sem("rms_ready")
        out_raw, out_done = sem("out_raw"), sem("out_done")
        dve_step, act_step = sem("dve_step"), sem("act_step")
        s = {n: sem(n) for n in (
            "wba_hi", "wba_ready", "ba_prod", "ba_cross", "ba_sum", "beta", "softplus", "g", "gc_prod", "gates",
            "qkvz_raw", "qkvz_ready", "uv_ready",
            "tok", "tok_sq", "ss", "root", "normed", "q_decayed", "lg", "gb", "elast", "kb_copy", "decay_in", "decay",
            "feat_dve", "feat", "feat_act", "attn", "attn_copy", "inv0", "t_prod",
            "t_copy", "y_prod", "z", "ut_prod", "u_copy",
            "w_prod", "w_copy",
            "v_prod", "v_copy", "s_prod", "state",
            "o_sq", "o_ss", "o_root", "o_norm", "o_prod", "gated", "mix_hi", "mix_a",
            "gv_prod", "gv_center", "gv_sq", "gv_ss", "gv_root", "gv_norm", "mixed", "gm_out", "gm_hi", "mix_b",
            "glu_scaled", "gate", "taps0", "taps1", "pivot_sum", "pivot", "acc_init", "first_ln_d", "ln_sq", "ln_stats",
            "ln_var", "ln_root", "ln_norm", "ln_act", "gained")}
        block = ctx.enter_context(nc.Block())

        slots = [x_space[:, i, :] for i in range(8)] + [work[:, 8192 + 512 * i:8192 + 512 * i + 512] for i in range(8)]
        buf = {n: slots[i].rearrange("p (h c) -> p h c", h=HH) for i, n in enumerate(
            ["lg", "kn", "qn", "vb", "kb", "kd", "kt", "qd", "knT", "kbT", "qnT", "qdT", "decay", "attnT", "state",
             "decay_s"])}
        for later, first in (("sq_k", "knT"), ("sq_q", "kbT"), ("C", "kn"), ("U", "qn"), ("T", "kb"), ("Z", "knT"),
                             ("wT", "kbT"), ("v_new", "qnT"), ("state_d", "decay_s"), ("o_sq", "decay"), ("o_n", "kd"),
                             ("gate_out", "kt")):
            buf[later] = buf[first]
        u_act, v_act = (acts[:, 2 * i:2 * i + 2, :] for i in range(2))
        v_rows, v_sq = (acts[:, 8 + 2 * i:10 + 2 * i, :].rearrange("p g (m c) -> p (g m) c", m=TT) for i in range(2))
        ln_g2, ln_b2, b_s2, w_s2 = (acts[:, 16 + i, :].rearrange("p (g c) -> p g c", g=2) for i in range(4))
        elast = small[:, 0:4].rearrange("p a m h -> p (a m h)")[:, 0:8].rearrange("p (h c) -> p h c", c=2)
        flat_small = small[:].rearrange("p a m h -> p (a m h)")

        def sm(i, n=8):
            return flat_small[:, 16 + 8 * i:16 + 8 * i + n]

        def advance(stream, quarter):
            while stream["next"] <= quarter:
                stream["next"] = next(stream["steps"], NEVER)

        def stream(steps):
            return {"steps": steps, "next": 0}

        def twice(ap):
            return ap.unsqueeze(2).to_broadcast([P, 2, TT, P])

        def tok(m):
            return slice(P * m, P * m + P)

        @block.sync
        def _(sp):
            sp.dma_start(pt[:], params).then_inc(const_in, 16)
            for j in range(4):
                sp.dma_start(x[:, 4 * j:4 * j + 4, :], xt[:, 4 * j:4 * j + 4, :]).then_inc(x_in[j], 16)
                if j < RAW:
                    sp.dma_start(raw[:, j, :], wts[j]).then_inc(raw_in[j], 16)

            def split_chunk(i, r):
                sp.wait_ge(lo_ready, 2 * (RAW * i + r - RAW + 1))
                sp.dma_start(raw[:, r, :], wts[RAW * i + r]).then_inc(raw_in[r], 16)

            split_chunk(1, 0)
            for dst, src in ((ct[:], consts), (wba_raw[:], w_ba), (cw[:], conv_w)):
                sp.dma_start(dst, src).then_inc(table_in, 16)
            split_chunk(1, 1)
            sp.dma_start(dwt[:], dw).then_inc(dw_in, 16)
            with sp.Fori(2, 2 * G_PW1 + 1) as i:
                for r in range(RAW):
                    split_chunk(i, r)
            with sp.Fori(2 * G_PW1 + 1, 2 * G_PW2 + 1) as i:
                for r in range(RAW):
                    sp.wait_ge(raw_used, RAW * i + r - RAW + 1 - 4 * G_PW1)
                    sp.dma_start(raw[:, r, :], wts[RAW * i + r]).then_inc(raw_in[r], 16)
            with sp.Fori(2 * G_PW2 + 1, 2 * G_END) as i:
                for r in range(RAW):
                    sp.wait_ge(lo_ready, 2 * (RAW * i + r - RAW + 1) - 8 * UNSPLIT)
                    sp.dma_start(raw[:, r, :], wts[RAW * i + r]).then_inc(raw_in[r], 16)

        @block.gpsimd
        def _(pool):
            for i in range(4):
                if i == 0:
                    pool.wait_ge(s["tok"], 2)
                else:
                    pool.wait_ge(s["gm_out"], i)
                for n, dst in enumerate((ln_g2, ln_b2, b_s2)):
                    pool.dma_start(dst.rearrange("p g c -> p (g c)"),
                                   rows[n:n + 1, 256 * i:256 * i + 256].to_broadcast([P, 256])).then_inc(rows_in, 16)
                pool.dma_start(w_s2.rearrange("p g c -> p (g c)"), w_s[:, 256 * i:256 * i + 256]).then_inc(rows_in, 16)
            pool.wait_ge(s["mix_a"], 4)
            pool.dma_start(x[:], xt).then_inc(x_again, 16)
            for j in range(4):
                pool.wait_ge(out_raw, j + 1)
                pool.dma_start(out[:, CH_K * j:CH_K * j + CH_K, :], conv[:, CH_K * j:CH_K * j + CH_K, :]).then_inc(out_done, 16)
            pool.wait_ge(out_done, 64)

        @block.scalar
        def _(act):
            side = []

            def copy(dst, src):
                return nc.scalar.activation(dst, src, ACT.Copy)

            def high_part(G, i, skipped=0):
                r = i // 2 % RAW
                act.wait_ge(raw_in[r], 16 * (2 * G + i // 4 + 1))
                act.wait_ge(half_free, 8 * (G - skipped) + i + 1)
                nc.scalar.activation(whi[:, i % SPLIT].rearrange("p a b -> p (a b)"),
                                     raw[:, r, HALF * (i % 2):HALF * (i % 2) + HALF], ACT.Copy).then_inc(hi_ready, 1)

            def split(G, *ks, skipped=0):
                for k in ks:
                    if splits_on(G, k):
                        high_part(G, 11 + k, skipped)
                    if side:
                        side_work(16 * G + 16 + 2 * k)

            def side_work(quarter):
                for q in range(quarter, quarter + 2):
                    for st in side:
                        advance(st, q)

            def copy_cross(G, par, bias=None, skipped=0):
                act.wait_ge(half_free, SPLIT + 8 * (G - skipped) + 8)
                act.wait_ge(banks_free, G + 2)
                if isinstance(G, int) and G == G_MLP0:
                    act.wait_ge(s["mix_b"], 4)
                src = ps[:, 4 * par:4 * par + 4, T:2 * T]
                if bias is None:
                    copy(cross[:], src).then_inc(cross_ready, 1)
                    return
                for t in range(CH_K):
                    ins = nc.scalar.activation(cross[:, t, :], src[:, t, :], ACT.Identity, bias=bias[:, t:t + 1])
                ins.then_inc(cross_ready, 1)

            def norm_part(e, j, xw):
                if 4 <= e < 8:
                    act.wait_ge(banks_free, G_WOUT + e - 4 + 3)
                elif e >= 8:
                    act.wait_ge(x_new, e - 7)
                if e:
                    act.wait_ge(ssum_part, e)
                nc.scalar.activation(padded[:, :, 0:T], xw, ACT.Square).then_inc(sq_ready, 1)
                if j is not None:
                    act.wait_ge(xg_raw, e + 1)
                    copy(xg[:, 4 * j:4 * j + 4, 0, :], total[:]).then_inc(xg_hi, 1)

            def root(n):
                act.wait_ge(ms_ready, n + 1)
                nc.scalar.activation(sq_part[:], ps[:, 7, 0:T], ACT.Sqrt, scale=1.0 / D, bias=eps).then_inc(root_ready, 1)

            eps, eps_q = param("eps"), param("eps_q")
            gate_bias = param("pw1_b")[:, KT:2 * KT]
            act.wait_ge(const_in, 16)
            for j in range(4):
                act.wait_ge(xg_raw, j + 1)
                copy(xg[:, 4 * j:4 * j + 4, 0, :], total[:]).then_inc(xg_hi, 1)
                for i in range(2 * j, 2 * j + 2):
                    high_part(0, i)
            for j in range(4):
                act.wait_ge(x_in[j], 16)
                if j:
                    act.wait_ge(ssum_part, j)
                nc.scalar.activation(padded[:, :, 0:T], x[:, 4 * j:4 * j + 4, :], ACT.Square).then_inc(sq_ready, 1)
                if j < 3:
                    high_part(0, 8 + j)
            act.wait_ge(table_in, 48)
            copy(wba[:, :, 0, :], wba_raw[:]).then_inc(s["wba_hi"], 1)
            split(0, 0)
            root(0)

            def qkvz(G):
                split(G, *range(G == 0, 4))
                t0 = QKVZ_AT[G]
                if t0 >= 24:
                    act.wait_ge(banks_free, G + 3)
                else:
                    act.wait_ge(s["qkvz_raw"], G - G // 4 + 1)
                nc.scalar.activation(acts[:, t0:t0 + 4, :], acts[:, t0:t0 + 4, :], ACT.Silu).then_inc(s["qkvz_ready"], 1)
                split(G, 4, 5, 6, 7)

            def gate_steps():
                yield GATES_START + 1
                act.wait_ge(s["ba_prod"], 1)
                copy(flat_small[:, 0:32].rearrange("p (m c) -> p m c", m=TT),
                     ps[:, 6, 0:128].rearrange("p (m c) -> p m c", m=TT)[:, :, NB:2 * NB]).then_inc(s["ba_cross"], 1)
                nc.scalar.activation(flat_small[:, 128:130], ps[:, 6, 128:130], ACT.Sqrt, scale=1.0 / D,
                                     bias=eps).then_inc(s["ba_cross"], 1)
                yield GATES_START + 5
                act.wait_ge(s["ba_sum"], 1)
                nc.scalar.activation(gates[:, 0], gates[:, 5], ACT.Sigmoid).then_inc(s["beta"], 1)
                nc.scalar.activation(gates[:, 1], gates[:, 6], ACT.Abs).then_inc(act_step, 1)
                yield GATES_START + 7
                act.wait_ge(act_step, 1)
                nc.scalar.activation(flat_small[:, 136:144], param("a_log"), ACT.Exp).then_inc(s["softplus"], 1)
                nc.scalar.activation(gates[:, 2], gates[:, 1], ACT.Exp, scale=-1.0).then_inc(act_step, 1)
                yield GATES_START + 9
                act.wait_ge(act_step, 2)
                nc.scalar.activation(gates[:, 1], gates[:, 2], ACT.Ln, bias=1.0).then_inc(s["softplus"], 1)
                yield GATES_START + 19
                act.wait_ge(s["g"], 2)
                nc.scalar.activation(gates[:, 3], gates[:, 2], ACT.Exp).then_inc(s["gates"], 1)
                nc.scalar.activation(gates[:, 4], gates[:, 4], ACT.Exp).then_inc(s["gates"], 1)

            qkvz(0)
            side = [stream(gate_steps())]
            qkvz(1)
            qkvz(2)

            def mixer_a():
                for b in range(4):
                    hh, m = b // 2, b % 2
                    start = BLOCK_START + BLOCK_TIME * b
                    yield start + AT["tok"] + 1
                    act.wait_ge(s["tok"], b + 1)
                    nc.scalar.activation(buf["sq_k"], bank(4), ACT.Square)
                    nc.scalar.activation(buf["sq_q"], bank(5), ACT.Square).then_inc(s["tok_sq"], 1)
                    yield start + AT["tok"] + 2
                    act.wait_ge(s["ss"], b + 1)
                    nc.scalar.activation(sm(1, 4), sm(0, 4), ACT.Sqrt, bias=eps)
                    nc.scalar.activation(sm(1, 8)[:, 4:8], sm(0, 8)[:, 4:8], ACT.Sqrt, scale=float(P), bias=eps_q).then_inc(s["root"], 1)
                    yield start + AT["gb"] + 1
                    act.wait_ge(s["gb"], b + 1)
                    nc.scalar.activation(elast, bank(4)[:, :, C - 1::C], ACT.Exp).then_inc(s["elast"], 1)
                    copy(buf["kbT"], bank(6)).then_inc(s["kb_copy"], 1)
                    act.wait_ge(s["decay_in"], b + 1)
                    nc.scalar.activation(buf["decay"], buf["lg"], ACT.Exp).then_inc(s["decay"], 1)
                    yield start + AT["feat"] + 1
                    act.wait_ge(s["feat"], b + 1)
                    copy(buf["qnT"], bank(4)).then_inc(s["feat_act"], 1)
                    copy(buf["qdT"], bank(5)).then_inc(s["feat_act"], 1)
                    yield start + AT["t_prod"] + 1
                    act.wait_ge(s["t_prod"], b + 1)
                    copy(buf["T"], bank(5)).then_inc(s["t_copy"], 1)
                    for lev in range(1, LEVELS):
                        yield start + AT["levels"] + 2 * lev
                        act.wait_ge(s["ut_prod"], LEVELS * b + lev)
                        copy(buf["T"], bank(5)).then_inc(s["t_copy"], 1)
                    yield start + AT["w"] + 1
                    act.wait_ge(s["w_prod"], b + 1)
                    nc.scalar.activation(buf["wT"], bank(6), ACT.Copy, scale=-1.0).then_inc(s["w_copy"], 1)
                    for cc in range(2):
                        R = slice(C * cc, C * cc + C)
                        yield start + AT["chunks"] + 2 * cc + 1
                        act.wait_ge(s["v_prod"], 2 * b + cc + 1)
                        copy(buf["v_new"][R], bank(6)[R]).then_inc(s["v_copy"], 1)
                    yield start + AT["chunks"] + 4
                    act.wait_ge(s["s_prod"], 2 * b + 2)
                    nc.scalar.activation(buf["o_sq"], bank(4), ACT.Square).then_inc(s["o_sq"], 1)
                    act.wait_ge(s["o_ss"], b + 1)
                    nc.scalar.activation(sm(3, 4), sm(2, 4), ACT.Sqrt, scale=1.0 / P, bias=eps).then_inc(s["o_root"], 1)
                    yield start + AT["o"] + 1
                    act.wait_ge(s["gated"], b + 1)
                    copy(hid[:, 4 * hh:4 * hh + 4, 0, tok(m)], buf["gate_out"]).then_inc(s["mix_hi"], 1)

            def mixer_b():
                for i in range(4):
                    start = 16 * (G_UV + i + 1)
                    yield start + UV_ROWS + 2
                    act.wait_ge(s["gv_center"], i + 1)
                    nc.scalar.activation(v_sq, v_rows, ACT.Square).then_inc(s["gv_sq"], 1)
                    act.wait_ge(s["gv_ss"], i + 1)
                    nc.scalar.activation(sm(6, 4), sm(5, 4), ACT.Sqrt, scale=1.0 / P, bias=eps).then_inc(s["gv_root"], 1)
                    yield start + UV_MIX + 1
                    act.wait_ge(s["gm_out"], i + 1)
                    copy(hid[:, 8 + 2 * i:10 + 2 * i, 0, :], v_act).then_inc(s["gm_hi"], 1)

            side = [stream(mixer_a()), stream(mixer_b())]
            for G in range(3, G_UV):
                qkvz(G)
            for G in range(G_UV, G_WOUT):
                i = G - G_UV
                split(G, 0)
                act.wait_ge(banks_free, G + 3)
                if i:
                    act.wait_ge(s["mix_b"], i)
                else:
                    act.wait_ge(s["tok"], 2)
                nc.scalar.activation(u_act, total[:, 0:2, :], ACT.Gelu)
                nc.scalar.activation(v_act, total[:, 2:4, :], ACT.Gelu).then_inc(s["uv_ready"], 1)
                split(G, 1, 2, 3, 4, 5, 6, 7)
            act.wait_ge(x_again, 16)
            for j in range(4):
                G = G_WOUT + j
                split(G, 0, 1)
                norm_part(4 + j, j, x[:, 4 * j:4 * j + 4, :])
                split(G, 2, 3, 4, 5, 6, 7)
            side = []

            def mlp(base, layer, q, last, last_norm):
                skipped = UNSPLIT * layer
                for j in range(4):
                    G = base + 8 * q + j
                    copy_cross(G, j % 2, skipped=skipped)
                    split(G, 0, 1, 2, skipped=skipped)
                    n = 16 * layer + 4 * q + j
                    act.wait_ge(hid_raw, n + 1)
                    copy(hid[:, 4 * j:4 * j + 4, 0, :], padded[:, :, 0:T]).then_inc(hid_hi, 1)
                    split(G, 3, 4, 5, 6, 7, skipped=skipped)
                for j in range(4):
                    G = base + 8 * q + 4 + j
                    copy_cross(G, j % 2, skipped=skipped)
                    split(G, 0, 1, skipped=skipped)
                    if last:
                        e = 8 + 8 * layer + j
                        norm_part(e, None, x[:, 4 * j:4 * j + 4, :])
                    if last_norm:
                        for t in range(4 * j, 4 * j + 4):
                            ins = nc.scalar.activation(conv[:, t, :], x[:, t, :], ACT.Copy,
                                                       scale=param("final_norm")[:, t:t + 1])
                        ins.then_inc(s["gained"], 1)
                    split(G, 2, 3, 4, 5, 6, 7, skipped=skipped)

            root(1)
            with act.Fori(0, NQ - 1) as q:
                mlp(G_MLP0, 0, q, False, False)
            mlp(G_MLP0, 0, NQ - 1, True, False)

            root(2)

            def gate(i, par):
                act.wait_ge(s["glu_scaled"], 2 * i + par + 1)
                for t in range(2):
                    ins = nc.scalar.activation(total[:, 2 + t, :], total[:, 2 + t, :], ACT.Sigmoid,
                                               bias=gate_bias[:, bass.ds(4 * i + 2 * par + t, 1)])
                ins.then_inc(s["gate"], 1)

            def squares(n, tiles):
                act.wait_ge(s["taps0"], WD * n + WD)
                act.wait_ge(s["taps1"], WD * n + WD)
                nc.scalar.activation(xf[:, tiles, :], conv[:, tiles, :], ACT.Square).then_inc(s["ln_sq"], 1)

            gate(0, 0)
            gate(0, 1)
            act.wait_ge(s["pivot_sum"], 1)
            nc.scalar.activation(pivot, ps[:, 7, 0:T], ACT.Copy, scale=-1.0 / (2 * P)).then_inc(s["pivot"], 1)
            act.wait_ge(s["pivot"], 1)
            for t in range(4, KT):
                ins = nc.scalar.activation(conv[:, t, :], pivot, ACT.Identity, bias=param("dw_b")[:, t:t + 1])
            ins.then_inc(s["acc_init"], 1)
            with act.Fori(1, 4) as i:
                for par in range(2):
                    gate(i, par)
            act.wait_ge(raw_used, 4 * UNSPLIT)
            act.wait_ge(s["first_ln_d"], 1)
            squares(1, slice(0, 4))
            squares(3, slice(4, 8))
            squares(5, slice(8, 12))
            for i in range(4):
                high_part(G_PW2, i, UNSPLIT)
            squares(6, slice(12, 14))
            squares(7, slice(14, 16))
            act.wait_ge(s["ln_var"], 1)
            nc.scalar.activation(sq_part[:], sq_part[:], ACT.Sqrt, bias=eps).then_inc(s["ln_root"], 1)
            for j in range(4):
                act.wait_ge(s["ln_norm"], j + 1)
                for t in range(4 * j, 4 * j + 4):
                    ins = nc.scalar.activation(conv[:, t, :], conv[:, t, :], ACT.Silu, scale=param("ln_g")[:, t:t + 1],
                                               bias=param("ln_b")[:, t:t + 1])
                ins.then_inc(s["ln_act"], 1)
                act.wait_ge(s["ln_act"], j + 1)
                copy(hid[:, 4 * j:4 * j + 4, 0, :], conv[:, 4 * j:4 * j + 4, :]).then_inc(hid_hi, 1)
                if j:
                    for i in range(2 * j + 2, 2 * j + 4):
                        high_part(G_PW2, i, UNSPLIT)
            high_part(G_PW2, 10, UNSPLIT)
            for j in range(4):
                G = G_PW2 + j
                copy_cross(G, G % 2, bias=param("pw2_b")[:, 4 * j:4 * j + 4], skipped=UNSPLIT)
                split(G, 0, 1, skipped=UNSPLIT)
                norm_part(12 + j, j, x[:, 4 * j:4 * j + 4, :])
                split(G, 2, 3, 4, 5, 6, 7, skipped=UNSPLIT)

            root(3)
            with act.Fori(0, NQ - 1) as q:
                mlp(G_MLP1, 1, q, False, False)
            mlp(G_MLP1, 1, NQ - 1, True, True)
            root(4)

        @block.vector
        def _(dve):
            tt = nc.vector.tensor_tensor
            stt = nc.vector.scalar_tensor_tensor
            chain = [0]
            side = []

            def link(ins):
                chain[0] += 1
                ins.then_inc(dve_step, 1)
                dve.wait_ge(dve_step, chain[0])

            def low_part(G, i, skipped=0):
                dve.wait_ge(hi_ready, 8 * (G - skipped) + i + 1)
                tt(wlo[:, i % SPLIT].rearrange("p a b -> p (a b)"),
                   raw[:, i // 2 % RAW, HALF * (i % 2):HALF * (i % 2) + HALF],
                   whi[:, i % SPLIT].rearrange("p a b -> p (a b)").bitcast(F32), ALU.subtract).then_inc(lo_ready, 1)

            def split(G, *ks, skipped=0):
                for k in ks:
                    if splits_on(G, k):
                        low_part(G, 11 + k, skipped)
                    if side:
                        side_work(16 * G + 16 + 2 * k)

            def side_work(quarter):
                for q in range(quarter, quarter + 2):
                    for st in side:
                        advance(st, q)

            def leave_psum(G, par, skipped=0):
                dve.wait_ge(cross_ready, G - G_MLP0 - skipped + 1)
                tt(total[:], ps[:, 4 * par:4 * par + 4, 0:T], cross[:], ALU.add).then_inc(banks_free, 1)
                dve.wait_ge(banks_free, G + 3)

            def products(G):
                dve.wait_ge(half_free, SPLIT + 8 * G + 8)
                return ps[:, NARROW_BANK[G]:NARROW_BANK[G] + 2, :].rearrange("p b (n t) -> p (b n) t", t=T)

            def by_token(ap, n):
                return ap.unsqueeze(1).to_broadcast([P, n, T])

            def norm_part(e, j, gain, first, G=None, unsplit=False, skipped=0):
                xw = x[:, 4 * j:4 * j + 4, :]
                if gain is not None:
                    g = param(gain)[:, 4 * j:4 * j + 4].unsqueeze(2).to_broadcast([P, 4, T])
                    tt(xf[:, 4 * j:4 * j + 4, :] if unsplit else total[:], xw, g, ALU.mult).then_inc(xg_raw, 1)
                if G is not None:
                    split(G, 2, skipped=skipped)
                dve.wait_ge(sq_ready, e + 1)
                squares = padded[:, :, 0:T].rearrange("p n t -> p t n")
                nc.vector.tensor_reduce(ssum[:] if first else sq_part[:], squares, AX, ALU.add).then_inc(ssum_part, 1)
                dve.wait_ge(ssum_part, e + 1)
                if j == 3:
                    tt(ssum[:], ssum[:], sq_part[:], ALU.add).then_inc(ssum_ready, 1)
                    dve.wait_ge(ssum_ready, e // 4 + 1)
                elif j:
                    link(tt(ssum[:], ssum[:], sq_part[:], ALU.add))
                if G is not None:
                    split(G, 3, skipped=skipped)
                if gain is not None and not unsplit:
                    hi_parts = e + 1 - (4 if e >= 12 else 0)
                    dve.wait_ge(xg_hi, hi_parts)
                    tt(xg[:, 4 * j:4 * j + 4, 1, :], total[:], xg[:, 4 * j:4 * j + 4, 0, :].bitcast(F32),
                       ALU.subtract).then_inc(xg_ready, 1)
                    dve.wait_ge(xg_ready, hi_parts)
                if G is not None:
                    split(G, 4, 5, 6, 7, skipped=skipped)

            def rms_of(n):
                dve.wait_ge(root_ready, n + 1)
                nc.vector.reciprocal(rms[:], sq_part[:]).then_inc(rms_ready, 1)
                dve.wait_ge(rms_ready, n + 1)

            dve.wait_ge(const_in, 16)
            for j in range(4):
                dve.wait_ge(x_in[j], 16)
                g = param("e_norm")[:, 4 * j:4 * j + 4].unsqueeze(2).to_broadcast([P, 4, T])
                tt(total[:], x[:, 4 * j:4 * j + 4, :], g, ALU.mult).then_inc(xg_raw, 1)
                dve.wait_ge(xg_hi, j + 1)
                tt(xg[:, 4 * j:4 * j + 4, 1, :], total[:], xg[:, 4 * j:4 * j + 4, 0, :].bitcast(F32),
                   ALU.subtract).then_inc(xg_ready, 1)
                dve.wait_ge(xg_ready, j + 1)
                for i in range(2 * j, 2 * j + 2):
                    low_part(0, i)
            for j in range(4):
                norm_part(j, j, None, j == 0)
                if j < 3:
                    low_part(0, 8 + j)
            dve.wait_ge(s["wba_hi"], 1)
            tt(wba[:, :, 1, :], wba_raw[:], wba[:, :, 0, :].bitcast(F32), ALU.subtract).then_inc(s["wba_ready"], 1)
            split(0, 0)
            link(nc.vector.memset(padded[:, :, 0:3], 0.0))
            rms_of(0)

            def qkvz(G):
                t0 = QKVZ_AT[G]
                if t0 >= 24:
                    ins = tt(acts[:, t0:t0 + 4, :], products(G), by_token(rms[:], 4), ALU.mult)
                    ins.then_inc(banks_free, 1)
                    dve.wait_ge(banks_free, G + 3)
                    split(G, 0, 1, 2, 3, 4, 5, 6, 7)
                    return
                if G:
                    dve.wait_ge(s["qkvz_raw"], G - G // 4)
                tt(padded[:, :, 3:3 + T], products(G), by_token(rms[:], 4), ALU.mult).then_inc(banks_free, 1)
                dve.wait_ge(banks_free, G + 3)
                for k in range(4):
                    if G or k:
                        split(G, k)
                    for t in range(4):
                        w = cw[:, t0 + t, k:k + 1]
                        dst, src = acts[:, t0 + t, :], padded[:, t, k:k + T]
                        if k == 0:
                            ins = nc.vector.tensor_scalar(dst, src, w, None, ALU.mult)
                        else:
                            ins = stt(dst, src, w, dst, ALU.mult, ALU.add)
                    if k < 3:
                        link(ins)
                ins.then_inc(s["qkvz_raw"], 1)
                split(G, 4, 5, 6, 7)

            def gate_steps():
                yield GATES_START + 3
                dve.wait_ge(s["ba_cross"], 2)
                ba = ps[:, 6, 0:128].rearrange("p (m c) -> p m c", m=TT)[:, :, 0:NB]
                crossed = flat_small[:, 0:32].rearrange("p (m c) -> p m c", m=TT)
                both = flat_small[:, 32:64].rearrange("p (m c) -> p m c", m=TT)
                tt(both, ba, crossed, ALU.add)
                link(nc.vector.reciprocal(flat_small[:, 130:132], flat_small[:, 128:130]))
                for m in range(TT):
                    nc.vector.tensor_scalar(gates[:, 5, m], both[:, m, 0:H], flat_small[:, 130 + m:131 + m], None, ALU.mult)
                    ins = stt(gates[:, 6, m], both[:, m, H:2 * H], flat_small[:, 130 + m:131 + m], param("dt_bias"),
                              ALU.mult, ALU.add)
                ins.then_inc(s["ba_sum"], 1)
                yield GATES_START + 11
                dve.wait_ge(s["softplus"], 2)
                link(stt(gates[:, 1], gates[:, 6], 0.0, gates[:, 1], ALU.max, ALU.add))
                stt(gates[:, 1], gates[:, 1], -1.0, flat_small[:, 136:144].unsqueeze(1).to_broadcast([P, TT, H]),
                    ALU.mult, ALU.mult).then_inc(s["g"], 1)
                yield GATES_START + 17
                dve.wait_ge(s["gc_prod"], 1)
                link(nc.vector.tensor_copy(gates[:, 2], ps[:, 6, 0:16].rearrange("p (m h) -> p m h", m=TT)))
                tt(gates[:, 4], ps[:, 6, 16:32].rearrange("p (m h) -> p m h", m=TT), gates[:, 2],
                   ALU.subtract).then_inc(s["g"], 1)

            qkvz(0)
            side = [stream(gate_steps())]
            qkvz(1)
            qkvz(2)

            def mixer_a():
                for b in range(4):
                    hh, m = b // 2, b % 2
                    start = BLOCK_START + BLOCK_TIME * b
                    heads = slice(HH * hh, HH * hh + HH)
                    beta, g, gc, eg, et = (gates[:, i, m, heads] for i in range(5))
                    yield start - 1
                    if b == 0:
                        dve.wait_ge(s["gates"], 2)
                    tt(buf["lg"], all_heads(const("upto")), per_head(g), ALU.mult).then_inc(s["lg"], 1)
                    yield start + AT["tok"] + 1
                    dve.wait_ge(s["tok_sq"], b + 1)
                    nc.vector.tensor_reduce(sm(0, 4), buf["sq_k"], AX, ALU.add)
                    nc.vector.tensor_reduce(sm(0, 8)[:, 4:8], buf["sq_q"], AX, ALU.add).then_inc(s["ss"], 1)
                    tt(buf["vb"], bank(6), per_head(beta), ALU.mult)
                    yield start + AT["tok"] + 3
                    dve.wait_ge(s["root"], b + 1)
                    link(nc.vector.reciprocal(sm(4), sm(1)))
                    tt(buf["kn"], bank(4), per_head(sm(4, 4)), ALU.mult)
                    link(tt(buf["qn"], bank(5), per_head(sm(4, 8)[:, 4:8]), ALU.mult))
                    tt(buf["kb"], buf["kn"], per_head(beta), ALU.mult).then_inc(s["normed"], 1)
                    yield start + AT["tok"] + 4
                    tt(buf["qd"], buf["qn"], per_head(eg), ALU.mult).then_inc(s["q_decayed"], 1)
                    tt(buf["kt"], buf["kn"], per_head(et), ALU.mult)
                    yield start + AT["gb"] + 1
                    dve.wait_ge(s["elast"], b + 1)
                    link(tt(buf["lg"], bank(4), per_head(gc), ALU.subtract))
                    tt(buf["lg"], buf["lg"], all_heads(const("fill")), ALU.min).then_inc(s["decay_in"], 1)
                    nc.vector.tensor_copy(buf["knT"], bank(5)).then_inc(s["feat_dve"], 1)
                    dve.wait_ge(s["normed"], b + 1)
                    tt(buf["kd"], buf["kb"], per_head(eg), ALU.mult)
                    yield start + AT["feat"] + 1
                    dve.wait_ge(s["decay"], b + 1)
                    link(tt(buf["decay_s"], buf["decay"], all_heads(const("strict")), ALU.mult))
                    dve.wait_ge(s["feat"], b + 1)
                    link(tt(buf["C"], bank(6), buf["decay_s"], ALU.mult))
                    link(tt(buf["C"], buf["C"], all_heads(const("ident")), ALU.add))
                    tt(buf["U"], buf["C"], all_heads(const("lev0t")), ALU.mult).then_inc(s["inv0"], 1)
                    yield start + AT["attn"] + 1
                    dve.wait_ge(s["attn"], b + 1)
                    tt(buf["attnT"], bank(4), buf["decay"], ALU.mult).then_inc(s["attn_copy"], 1)
                    for lev in range(1, LEVELS + 1):
                        yield start + AT["levels"] + 2 * lev - 1
                        dve.wait_ge(s["y_prod"], LEVELS * b + lev)
                        tt(buf["Z"], bank(6), all_heads(const(f"lev{lev}")), ALU.mult).then_inc(s["z"], 1)
                        yield start + AT["levels"] + 2 * lev
                        dve.wait_ge(s["ut_prod"], LEVELS * b + lev)
                        nc.vector.tensor_copy(buf["U"], bank(4)).then_inc(s["u_copy"], 1)
                    if m == 0:
                        if b:
                            dve.wait_ge(s["state"], 5 * hh)
                        nc.vector.memset(buf["state"], 0.0).then_inc(s["state"], 1)
                    for cc in range(2):
                        if m == 0 or cc == 1:
                            dve.wait_ge(s["state"], 5 * hh + 2 * m + cc + 1)
                        link(tt(buf["state_d"], buf["state"], elast[:, :, cc].unsqueeze(2).to_broadcast([P, HH, P]), ALU.mult))
                        yield start + AT["chunks"] + 2 * cc + 2
                        dve.wait_ge(s["s_prod"], 2 * b + cc + 1)
                        tt(buf["state"], bank(5), buf["state_d"], ALU.add).then_inc(s["state"], 1)
                    dve.wait_ge(s["o_sq"], b + 1)
                    nc.vector.tensor_reduce(sm(2, 4), buf["o_sq"], AX, ALU.add).then_inc(s["o_ss"], 1)
                    dve.wait_ge(s["o_root"], b + 1)
                    link(nc.vector.reciprocal(sm(7, 4), sm(3, 4)))
                    tt(buf["o_n"], bank(4), per_head(sm(7, 4)), ALU.mult).then_inc(s["o_norm"], 1)
                    yield start + AT["o"] + 1
                    dve.wait_ge(s["o_prod"], b + 1)
                    z0 = 24 + HH * hh
                    dve.wait_ge(s["qkvz_ready"], 4 * hh + 4)
                    stt(buf["gate_out"], bank(6), param("head_norm"), acts[:, z0:z0 + HH, tok(m)], ALU.mult,
                        ALU.mult).then_inc(s["gated"], 1)
                    dve.wait_ge(s["mix_hi"], b + 1)
                    dst = hid[:, HH * hh:HH * hh + HH, :, tok(m)]
                    tt(dst[:, :, 1, :], buf["gate_out"], dst[:, :, 0, :].bitcast(F32), ALU.subtract).then_inc(s["mix_a"], 1)
                    dve.wait_ge(s["mix_a"], b + 1)

            def mixer_b():
                by_row = lambda ap: ap.unsqueeze(2).to_broadcast([P, 2 * TT, P])
                four = lambda ap: ap.rearrange("p (g m) c -> p g m c", m=TT)
                for i in range(4):
                    start = 16 * (G_UV + i + 1)
                    yield start + UV_ROWS + 1
                    dve.wait_ge(s["gv_prod"], i + 1)
                    link(nc.vector.tensor_reduce(sm(8, 4), bank(7), AX, ALU.add))
                    link(nc.vector.tensor_scalar(sm(8, 4), sm(8, 4), 1.0 / P, None, ALU.mult))
                    tt(v_rows, bank(7), by_row(sm(8, 4)), ALU.subtract).then_inc(s["gv_center"], 1)
                    yield start + UV_ROWS + 2
                    dve.wait_ge(rows_in, 64 * (i + 1))
                    link(nc.vector.memset(w_s2[C:P, :, 0:C], 0.0))
                    dve.wait_ge(s["gv_sq"], i + 1)
                    nc.vector.tensor_reduce(sm(5, 4), v_sq, AX, ALU.add).then_inc(s["gv_ss"], 1)
                    yield start + UV_ROWS + 4
                    dve.wait_ge(s["gv_root"], i + 1)
                    link(nc.vector.reciprocal(sm(9, 4), sm(6, 4)))
                    link(tt(v_rows, v_rows, by_row(sm(9, 4)), ALU.mult))
                    link(tt(four(v_rows), four(v_rows), twice(ln_g2), ALU.mult))
                    tt(four(v_rows), four(v_rows), twice(ln_b2), ALU.add).then_inc(s["gv_norm"], 1)
                    yield start + UV_MIX + 1
                    dve.wait_ge(s["mixed"], i + 1)
                    mixed = v_act.rearrange("p g (m c) -> p g m c", m=TT)
                    link(tt(mixed, four(bank(7)), twice(b_s2), ALU.add))
                    tt(v_act, v_act, u_act, ALU.mult).then_inc(s["gm_out"], 1)
                    dve.wait_ge(s["gm_hi"], i + 1)
                    dst = hid[:, 8 + 2 * i:10 + 2 * i, :, :]
                    tt(dst[:, :, 1, :], v_act, dst[:, :, 0, :].bitcast(F32), ALU.subtract).then_inc(s["mix_b"], 1)

            side = [stream(mixer_a()), stream(mixer_b())]
            for G in range(3, G_UV):
                qkvz(G)
            for G in range(G_UV, G_WOUT):
                if G > G_UV:
                    dve.wait_ge(s["uv_ready"], G - G_UV)
                tt(total[:], products(G), by_token(rms[:], 4), ALU.mult).then_inc(banks_free, 1)
                dve.wait_ge(banks_free, G + 3)
                split(G, 0, 1, 2, 3, 4, 5, 6, 7)

            dve.wait_ge(s["uv_ready"], 4)
            dve.wait_ge(x_again, 16)
            for j in range(4):
                G = G_WOUT + j
                w = x[:, 4 * j:4 * j + 4, :]
                tt(w, w, products(G), ALU.add).then_inc(banks_free, 1)
                dve.wait_ge(banks_free, G + 3)
                split(G, 0, 1)
                norm_part(4 + j, j, "f_norm0", j == 0, G)
            side = []

            def onto_residual(G, par, j, e, gain, part=0, skipped=0):
                leave_psum(G, par, skipped)
                split(G, 0, skipped=skipped)
                ins = tt(x[:, 4 * j:4 * j + 4, :], x[:, 4 * j:4 * j + 4, :], total[:], ALU.add)
                if e is not None:
                    ins.then_inc(x_new, 1)
                    dve.wait_ge(x_new, e - 7)
                    split(G, 1, skipped=skipped)
                    norm_part(e, j, gain, j == 0, G, gain == "o_norm", skipped)
                else:
                    ins.then_inc(x_part, 1)
                    dve.wait_ge(x_part, part + 1)
                    split(G, 1, 2, 3, 4, 5, 6, 7, skipped=skipped)

            def mlp(base, layer, q, last, gain):
                skipped = UNSPLIT * layer
                for j in range(4):
                    G = base + 8 * q + j
                    n = 16 * layer + 4 * q + j
                    leave_psum(G, j % 2, skipped)
                    split(G, 0, skipped=skipped)
                    tt(total[:], total[:], by_token(rms[:], 4), ALU.mult).then_inc(hid_scaled, 1)
                    split(G, 1, skipped=skipped)
                    dve.wait_ge(hid_scaled, n + 1)
                    stt(padded[:, :, 0:T], total[:], 0.0, total[:], ALU.max, ALU.mult).then_inc(hid_raw, 1)
                    split(G, 2, skipped=skipped)
                    dve.wait_ge(hid_hi, n + 4 * layer + 1)
                    tt(hid[:, 4 * j:4 * j + 4, 1, :], padded[:, :, 0:T], hid[:, 4 * j:4 * j + 4, 0, :].bitcast(F32),
                       ALU.subtract).then_inc(hid_ready, 1)
                    dve.wait_ge(hid_ready, n + 4 * layer + 1)
                    split(G, 3, 4, 5, 6, 7, skipped=skipped)
                for j in range(4):
                    G = base + 8 * q + 4 + j
                    onto_residual(G, j % 2, j, 8 + 8 * layer + j if last else None, gain, 12 * layer + 4 * q + j,
                                  skipped)

            rms_of(1)
            with dve.Fori(0, NQ - 1) as q:
                mlp(G_MLP0, 0, q, False, None)
            mlp(G_MLP0, 0, NQ - 1, True, "o_norm")

            rms_of(2)
            link(nc.vector.memset(zwin[:, :, 0:32], 0.0))
            dve.wait_ge(dw_in, 16)

            def convolve(i, par, first):
                n = 2 * i + par
                dve.wait_ge(raw_used, 4 * n + 4)
                tt(total[:], ps[:, 4 * par:4 * par + 4, 0:T], by_token(rms[:], 4), ALU.mult).then_inc(s["glu_scaled"], 1)
                dve.wait_ge(s["gate"], n + 1)
                tile0 = 4 * i + 2 * par
                z = [zwin[:, 2 * par + t, :] for t in range(2)]
                acc = [conv[:, bass.ds(tile0 + t, 1), :].rearrange("p a t -> p (a t)") for t in range(2)]
                for t in range(2):
                    ins = stt(z[t][:, 32:32 + T], total[:, t, :], param("pw1_b")[:, bass.ds(tile0 + t, 1)],
                              total[:, 2 + t, :], ALU.add, ALU.mult)
                ins.then_inc(banks_free, 1)
                dve.wait_ge(banks_free, G_PW1 + n + 3)
                if not first:
                    dve.wait_ge(s["acc_init"], 1)
                for k in range(WD):
                    for t in range(2):
                        src = z[t][:, 2 + k:2 + k + T]
                        w = dwt[:, bass.ds(tile0 + t, 1), k:k + 1].rearrange("p a t -> p (a t)")
                        taps = s["taps0" if t == 0 else "taps1"]
                        if k == 0 and first:
                            ins = nc.vector.tensor_scalar(acc[t], src, w, param("dw_b")[:, bass.ds(tile0 + t, 1)],
                                                          ALU.mult, ALU.add)
                        else:
                            if k:
                                dve.wait_ge(taps, WD * n + k)
                            ins = stt(acc[t], src, w, acc[t], ALU.mult, ALU.add)
                        ins.then_inc(taps, 1)

            for par in range(2):
                convolve(0, par, True)
            convolve(1, 0, False)
            dve.wait_ge(s["taps1"], 2 * WD)
            dve.wait_ge(s["taps0"], 2 * WD)
            tt(conv[:, 0:4, :], conv[:, 0:4, :], by_token(pivot, 4), ALU.add).then_inc(s["first_ln_d"], 1)
            convolve(1, 1, False)
            with dve.Fori(2, 4) as i:
                for par in range(2):
                    convolve(i, par, False)
            for i in range(4):
                low_part(G_PW2, i, UNSPLIT)
            dve.wait_ge(s["ln_stats"], 1)
            mean, mean_sq = total[:, 0, :], total[:, 1, :]
            link(nc.vector.tensor_scalar(mean, ps[:, 0, 0:T], 1.0 / D, None, ALU.mult))
            link(tt(mean_sq, mean, mean, ALU.mult))
            link(stt(sq_part[:], ps[:, 1, 0:T], 1.0 / D, mean_sq, ALU.mult, ALU.subtract))
            nc.vector.tensor_scalar(sq_part[:], sq_part[:], 0.0, None, ALU.max).then_inc(s["ln_var"], 1)

            def center(j):
                w = conv[:, 4 * j:4 * j + 4, :]
                link(tt(w, w, by_token(mean, 4), ALU.subtract))

            def normalize(j):
                w = conv[:, 4 * j:4 * j + 4, :]
                tt(w, w, by_token(rms[:], 4), ALU.mult).then_inc(s["ln_norm"], 1)

            def low_half(j):
                dve.wait_ge(hid_hi, 17 + j)
                tt(hid[:, 4 * j:4 * j + 4, 1, :], conv[:, 4 * j:4 * j + 4, :], hid[:, 4 * j:4 * j + 4, 0, :].bitcast(F32),
                   ALU.subtract).then_inc(hid_ready, 1)

            center(0)
            dve.wait_ge(s["ln_root"], 1)
            link(nc.vector.reciprocal(rms[:], sq_part[:]))
            normalize(0)
            for j in range(4):
                if j < 3:
                    center(j + 1)
                    normalize(j + 1)
                low_half(j)
                if j:
                    for i in range(2 * j + 2, 2 * j + 4):
                        low_part(G_PW2, i, UNSPLIT)
            low_part(G_PW2, 10, UNSPLIT)
            for j in range(4):
                onto_residual(G_PW2 + j, j % 2, j, 12 + j, "f_norm1", skipped=UNSPLIT)

            rms_of(3)
            with dve.Fori(0, NQ - 1) as q:
                mlp(G_MLP1, 1, q, False, None)
            mlp(G_MLP1, 1, NQ - 1, True, None)
            rms_of(4)
            for j in range(4):
                dve.wait_ge(s["gained"], j + 1)
                w = conv[:, 4 * j:4 * j + 4, :]
                tt(w, w, by_token(rms[:], 4), ALU.mult).then_inc(out_raw, 1)

        @block.tensor
        def _(pe):
            mm = nc.tensor.matmul

            def narrow_group(G, operand, ready):
                pe.wait_ge(banks_free, G + 1)
                for i in range(8):
                    pe.wait_ge(lo_ready, 8 * G + i + 1)
                    ready(i)
                    r = i % SPLIT
                    for k in range(CH_K // 2):
                        kt = CH_K // 2 * i + k
                        for n in range(4):
                            cols = slice(P * n, P * n + P)
                            dst = ps[:, NARROW_BANK[G] + n // 2, T * (n % 2):T * (n % 2) + T]
                            mm(dst, whi[:, r, k, cols], operand[:, kt, 0, :], start=(kt == 0 and n % 2 == 0), stop=False,
                               skip_group_check=True)
                            mm(dst, whi[:, r, k, cols], operand[:, kt, 1, :], start=False, stop=False,
                               skip_group_check=True)
                            ins = mm(dst, wlo[:, r, k, cols], operand[:, kt, 0, :], start=False, stop=(kt == KT - 1),
                                     skip_group_check=True)
                        if k == CH_K // 2 - 1:
                            ins.then_inc(half_free, 1)
                        for st in side:
                            advance(st, 16 * G + 2 * i + k)

            def group(G, par, operand, ready, counts, skipped=0, norm=None):
                pe.wait_ge(banks_free, G + 1)
                for i in range(8):
                    if norm is not None and i == 6:
                        mean_squares(norm, G)
                    pe.wait_ge(lo_ready, 8 * (G - skipped) + i + 1)
                    if ready is not None and i % 2 == 0:
                        pe.wait_ge(ready, counts + i // 2)
                    r = i % SPLIT
                    for k in range(CH_K // 2):
                        kt = CH_K // 2 * i + k
                        for n in range(4):
                            cols = slice(P * n, P * n + P)
                            mm(ps[:, 4 * par + n, :], whi[:, r, k, cols], operand[:, kt].rearrange("p a t -> p (a t)"),
                               start=(kt == 0), stop=False)
                            ins = mm(ps[:, 4 * par + n, T:2 * T], wlo[:, r, k, cols], operand[:, kt, 0, :],
                                     start=False, stop=(kt == KT - 1))
                    ins.then_inc(half_free, 1)

            def unsplit_group(G, par, norm=None, pivot=False):
                pe.wait_ge(banks_free, G + 1)
                for kc in range(4):
                    if norm is not None and kc == 3:
                        mean_squares(norm, G)
                    if pivot and kc == 3:
                        for t in range(2):
                            pe.wait_ge(s["taps0" if t == 0 else "taps1"], WD)
                        pe.wait_ge(banks_free, G + 2)
                        for t in range(2):
                            ins = mm(ps[:, 7, 0:T], const("ones"), conv[:, t, :], start=(t == 0), stop=(t == 1))
                        ins.then_inc(s["pivot_sum"], 1)
                    r = kc % RAW
                    pe.wait_ge(raw_in[r], 16 * (2 * G + kc // 2 + 1))
                    if norm is not None:
                        pe.wait_ge(xg_raw, 4 * norm + kc + 1)
                    for k in range(CH_K):
                        kt = CH_K * kc + k
                        for n in range(4):
                            ins = mm(ps[:, 4 * par + n, 0:T], raw[:, r, CH_N * k + P * n:CH_N * k + P * n + P],
                                     xf[:, kt, :], start=(kt == 0), stop=(kt == KT - 1))
                    ins.then_inc(raw_used, 1)

            def mean_squares(n, G=None):
                pe.wait_ge(ssum_ready, n + 1)
                if G is not None:
                    pe.wait_ge(banks_free, G + 2)
                mm(ps[:, 7, 0:T], const("ones"), ssum[:], start=True, stop=True).then_inc(ms_ready, 1)

            pe.sem_inc(half_free, SPLIT)
            pe.sem_inc(banks_free, 2)
            side = []

            def xg_tiles(i):
                pe.wait_ge(xg_ready, i // 2 + 1)

            def gate_products():
                yield 19
                mean_squares(0)
                for kt in range(KT):
                    yield 24 + kt // 2
                    if kt == 0:
                        pe.wait_ge(s["wba_ready"], 1)
                    for m in range(TT):
                        mm(ps[:, 6, 64 * m:64 * m + 2 * NB], xg[:, kt, 0, tok(m)],
                           wba[:, kt].rearrange("p a b -> p (a b)"), start=(kt == 0 and m == 0), stop=False,
                           skip_group_check=True)
                        mm(ps[:, 6, 64 * m + NB:64 * m + 2 * NB], xg[:, kt, 1, tok(m)], wba[:, kt, 0, :], start=False,
                           stop=(kt == KT - 1), skip_group_check=True)

            narrow_group(0, xg, xg_tiles)
            side = [stream(gate_products())]
            narrow_group(1, xg, xg_tiles)
            side = []
            for m in range(TT):
                ins = mm(ps[:, 6, 128 + m:129 + m], ssum[:, tok(m)], const("ones")[:, 0:1], start=True, stop=True)
            ins.then_inc(s["ba_prod"], 1)

            def decay_products():
                yield GATES_START + 14
                pe.wait_ge(s["g"], 1)
                mm(ps[:, 6, 0:16], const("upto"), gates[:, 1].rearrange("p m h -> p (m h)"), start=True, stop=True)
                mm(ps[:, 6, 16:32], const("chunk"), gates[:, 1].rearrange("p m h -> p (m h)"), start=True,
                   stop=True).then_inc(s["gc_prod"], 1)

            side = [stream(decay_products())]
            narrow_group(2, xg, xg_tiles)

            def transposes(b, src):
                for h in range(HH):
                    ins = nc.tensor.transpose(bank(b)[:, h, :], src(h), const("ident"))
                return ins

            def products(b, left, right):
                for h in range(HH):
                    ins = mm(bank(b)[:, h, :], left[:, h, :], right[:, h, :], start=True, stop=True)
                return ins

            def mixer_a():
                for b in range(4):
                    hh, m = b // 2, b % 2
                    start = BLOCK_START + BLOCK_TIME * b
                    yield start + AT["tok"]
                    pe.wait_ge(s["qkvz_ready"], 4 * hh + 3)
                    if b:
                        pe.wait_ge(s["gated"], b)
                        pe.wait_ge(s["state"], 5 * ((b - 1) // 2) + 2 * ((b - 1) % 2) + 3)
                    else:
                        pe.wait_ge(s["g"], 2)
                    transposes(4, lambda h: acts[:, 8 + HH * hh + h, tok(m)])
                    transposes(5, lambda h: acts[:, HH * hh + h, tok(m)])
                    transposes(6, lambda h: acts[:, 16 + HH * hh + h, tok(m)]).then_inc(s["tok"], 1)
                    yield start + AT["gb"]
                    pe.wait_ge(s["normed"], b + 1)
                    mm(ps[:, 4, :], const("ones"), buf["lg"].rearrange("p h c -> p (h c)"), start=True, stop=True)
                    transposes(5, lambda h: buf["kn"][:, h, :])
                    transposes(6, lambda h: buf["kb"][:, h, :]).then_inc(s["gb"], 1)
                    yield start + AT["feat"]
                    pe.wait_ge(s["feat_dve"], b + 1)
                    pe.wait_ge(s["kb_copy"], b + 1)
                    transposes(4, lambda h: buf["qn"][:, h, :])
                    transposes(5, lambda h: buf["qd"][:, h, :])
                    products(6, buf["knT"], buf["kbT"]).then_inc(s["feat"], 1)
                    yield start + AT["attn"]
                    pe.wait_ge(s["feat_act"], 2 * b + 2)
                    products(4, buf["knT"], buf["qnT"]).then_inc(s["attn"], 1)
                    yield start + AT["t_prod"]
                    pe.wait_ge(s["inv0"], b + 1)
                    transposes(5, lambda h: buf["U"][:, h, :]).then_inc(s["t_prod"], 1)
                    for lev in range(1, LEVELS + 1):
                        yield start + AT["levels"] + 2 * lev - 2
                        pe.wait_ge(s["t_copy"], LEVELS * b + lev)
                        if lev > 1:
                            pe.wait_ge(s["u_copy"], LEVELS * b + lev - 1)
                        products(6, buf["C"], buf["T"]).then_inc(s["y_prod"], 1)
                        yield start + AT["levels"] + 2 * lev - 1
                        pe.wait_ge(s["z"], LEVELS * b + lev)
                        if lev == 1:
                            pe.wait_ge(s["attn_copy"], b + 1)
                        ins = products(4, buf["Z"], buf["U"])
                        if lev < LEVELS:
                            ins = products(5, buf["U"], buf["Z"])
                        ins.then_inc(s["ut_prod"], 1)
                    yield start + AT["w"]
                    pe.wait_ge(s["u_copy"], LEVELS * b + LEVELS)
                    products(6, buf["kd"], buf["U"]).then_inc(s["w_prod"], 1)
                    for cc in range(2):
                        R = slice(C * cc, C * cc + C)
                        yield start + AT["chunks"] + 2 * cc
                        pe.wait_ge(s["w_copy"], b + 1)
                        pe.wait_ge(s["state"], 5 * hh + 2 * m + cc + 1)
                        for h in range(HH):
                            mm(bank(6)[R, h, :], buf["U"][:, h, R], buf["vb"][:, h, :], start=True, stop=False)
                            ins = mm(bank(6)[R, h, :], buf["wT"][:, h, R], buf["state"][:, h, :], start=False, stop=True)
                        ins.then_inc(s["v_prod"], 1)
                        yield start + AT["chunks"] + 2 * cc + 1
                        pe.wait_ge(s["v_copy"], 2 * b + cc + 1)
                        for h in range(HH):
                            mm(bank(4)[R, h, :], buf["qdT"][:, h, R], buf["state"][:, h, :], start=True, stop=False)
                            mm(bank(4)[R, h, :], buf["attnT"][R, h, R], buf["v_new"][R, h, :], start=False, stop=True)
                        for h in range(HH):
                            ins = mm(bank(5)[:, h, :], buf["kt"][R, h, :], buf["v_new"][R, h, :], start=True, stop=True)
                        ins.then_inc(s["s_prod"], 1)
                    yield start + AT["o"]
                    pe.wait_ge(s["o_norm"], b + 1)
                    transposes(6, lambda h: buf["o_n"][:, h, :]).then_inc(s["o_prod"], 1)

            def mixer_b():
                for i in range(4):
                    start = 16 * (G_UV + i + 1)
                    yield start + UV_ROWS
                    pe.wait_ge(s["uv_ready"], i + 1)
                    if i:
                        pe.wait_ge(s["gm_out"], i)
                    else:
                        pe.wait_ge(root_ready, 1)
                    for g in range(2):
                        for m in range(TT):
                            ins = nc.tensor.transpose(bank(7)[:, TT * g + m, :], v_act[:, g, tok(m)], const("ident"))
                    ins.then_inc(s["gv_prod"], 1)
                    yield start + UV_MIX
                    pe.wait_ge(s["gv_norm"], i + 1)
                    for g in range(2):
                        for m in range(TT):
                            ins = mm(bank(7)[:, TT * g + m, :], v_rows[:, TT * g + m, :], w_s2[:, g, :], start=True,
                                     stop=True)
                    ins.then_inc(s["mixed"], 1)

            side = [stream(mixer_a()), stream(mixer_b())]
            for G in range(3, G_WOUT):
                narrow_group(G, xg, lambda i: None)

            def mixed_tiles(i):
                if i < 4:
                    pe.wait_ge(s["mix_a"], 2 + 2 * (i // 2))
                else:
                    pe.wait_ge(s["mix_b"], i - 3)

            for G in range(G_WOUT, G_MLP0):
                narrow_group(G, hid, mixed_tiles)

            def mlp(base, layer):
                skipped, fours = UNSPLIT * layer, 4 * layer
                xg_count, norm = 5 + 4 * layer, 1 + 2 * layer
                for j in range(4):
                    group(base + j, j % 2, xg, xg_ready, xg_count, skipped, norm if j == 0 else None)
                    if j == 0:
                        pe.wait_ge(root_ready, norm + 1)
                with pe.Fori(0, 2) as i:
                    for par in range(2):
                        group(base + 4 + 2 * i + par, par, hid, hid_ready, 20 * layer + 1, skipped)
                with pe.Fori(1, NQ) as q:
                    with pe.Fori(0, 2) as i:
                        for par in range(2):
                            group(base + 8 * q + 2 * i + par, par, xg, None, 0, skipped)
                    with pe.Fori(0, 2) as i:
                        for par in range(2):
                            group(base + 8 * q + 4 + 2 * i + par, par, hid, hid_ready, 20 * layer + 4 * q + 1, skipped)

            mlp(G_MLP0, 0)
            unsplit_group(G_PW1, 0, norm=2)
            pe.wait_ge(root_ready, 3)
            unsplit_group(G_PW1 + 1, 1)
            unsplit_group(G_PW1 + 2, 0, pivot=True)
            pe.wait_ge(s["pivot"], 1)
            unsplit_group(G_PW1 + 3, 1)
            with pe.Fori(2, 4) as i:
                for par in range(2):
                    unsplit_group(G_PW1 + 2 * i + par, par)
            pe.wait_ge(banks_free, G_PW2 + 1)
            for step, tiles in enumerate((range(0, 4), range(4, 8), range(8, 12), range(12, 14), range(14, 16))):
                if step == 4:
                    for k in range(WARM):
                        pe.wait_ge(s["taps0"], WD * (UNSPLIT - 1) + WD * (k + 1) // (WARM + 1))
                        for _ in range(2):
                            mm(ps[:, 2, 0:T], const("ones"), xf[:, 0, :], start=True, stop=True)
                    pe.wait_ge(s["taps0"], WD * UNSPLIT)
                    pe.wait_ge(s["taps1"], WD * UNSPLIT)
                for b, src in ((0, conv), (1, xf)):
                    if b == 1 or step < 4:
                        pe.wait_ge(s["ln_sq"], step + 1)
                    for kt in tiles:
                        ins = mm(ps[:, b, 0:T], const("ones"), src[:, kt, :], start=(kt == 0), stop=(kt == KT - 1))
            ins.then_inc(s["ln_stats"], 1)
            for _ in range(2 * WARM):
                mm(ps[:, 2, 0:T], const("ones"), xf[:, 0, :], start=True, stop=True)
            pe.wait_ge(s["ln_root"], 1)
            with pe.Fori(0, 2) as i:
                for par in range(2):
                    group(G_PW2 + 2 * i + par, par, hid, hid_ready, 17, UNSPLIT)
            mlp(G_MLP1, 1)
            mean_squares(4)


_INS = ["xt", "wts", "w_ba", "consts", "params", "conv_w", "dw", "rows", "w_s"]


def tables():
    import numpy as np
    i = np.arange(P)
    same = i[:, None] // C == i[None, :] // C
    upto = same & (i[:, None] <= i[None, :])
    t = {"ident": np.eye(P), "ones": np.ones((P, P)), "upto": upto, "chunk": same,
         "fill": np.where(upto, 3e38, -3e38), "strict": upto & (i[:, None] < i[None, :])}
    for lev in range(LEVELS + 1):
        size = 1 << lev
        below = (i[:, None] // (2 * size) == i[None, :] // (2 * size)) & (i[:, None] // size > i[None, :] // size)
        m = np.eye(P) - below
        t["lev0t" if lev == 0 else f"lev{lev}"] = m.T if lev == 0 else m
    return np.ascontiguousarray(np.stack([t[n] for n in CONSTS], 1).astype(np.float32))


def kernel(**inputs):
    import numpy as np
    import concourse.bacc as bacc
    from concourse.bass_utils import run_bass_kernel_spmd as run

    a = {n: np.asarray(v) for n, v in inputs.items()}

    def chunks(w):
        w = w.reshape(4, CH_K, P, -1, CH_N)
        return w.transpose(3, 0, 2, 1, 4).reshape(-1, P, CH)

    def tiles(v):
        return v.reshape(-1, P).T

    w_in = a["e_w_in"][0]
    hd = H * P
    q, k, v, z = (w_in[:, i * hd:(i + 1) * hd] for i in range(4))
    ba = w_in[:, 4 * hd:4 * hd + NB]
    u, vr = (w_in[:, 4 * hd + NB + i * hd:4 * hd + NB + (i + 1) * hd] for i in range(2))
    half = CH_N
    cols = [w[:, part] for part in (slice(0, half), slice(half, None)) for w in (q, k, v, z)]
    for i in range(4):
        cols += [u[:, 256 * i:256 * i + 256], vr[:, 256 * i:256 * i + 256]]
    parts = [chunks(np.concatenate(cols, 1)), chunks(a["e_w_out"][0])]

    def mlp(layer):
        for i in range(NQ):
            parts.append(chunks(a["f_w1"][layer][:, i * D:(i + 1) * D]))
            parts.append(chunks(a["f_w2"][layer][i * D:(i + 1) * D]))

    mlp(0)
    pw1 = a["o_pw1"][0]
    cols = []
    for i in range(8):
        cols += [pw1[:, 256 * i:256 * i + 256], pw1[:, D + 256 * i:D + 256 * i + 256]]
    parts += [chunks(np.concatenate(cols, 1)), chunks(a["o_pw2"][0])]
    mlp(1)
    wide = lambda v: np.broadcast_to(v[None, :], (P, v.size))
    params = {"e_norm": tiles(a["e_norm"][0]), "f_norm0": tiles(a["f_norm"][0]), "o_norm": tiles(a["o_norm"][0]),
              "f_norm1": tiles(a["f_norm"][1]), "final_norm": tiles(a["final_norm"]), "pw1_b": tiles(a["o_pw1_b"][0]),
              "dw_b": tiles(a["o_dw_b"][0]), "ln_g": tiles(a["o_ln_g"][0]), "ln_b": tiles(a["o_ln_b"][0]),
              "pw2_b": tiles(a["o_pw2_b"][0]), "head_norm": tiles(a["e_o_norm"][0]), "a_log": wide(a["e_a_log"][0]),
              "dt_bias": wide(a["e_dt_bias"][0]), "eps": np.full((P, 1), EPS, np.float32),
              "eps_q": np.full((P, 1), EPS * P, np.float32)}
    arrays = {
        "xt": a["x"][0].T.reshape(KT, P, T).transpose(1, 0, 2),
        "wts": np.concatenate(parts, 0),
        "w_ba": ba.reshape(KT, P, NB).transpose(1, 0, 2),
        "consts": tables(),
        "params": np.concatenate([params[n] for n in PARAMS], 1),
        "conv_w": a["e_conv_w"][0].reshape(4, 24, P).transpose(2, 1, 0),
        "dw": a["o_dw"][0].reshape(WD, KT, P).transpose(2, 1, 0),
        "rows": np.stack([a["e_ln_g"][0], a["e_ln_b"][0], a["e_b_s"][0].reshape(-1)]),
        "w_s": a["e_w_s"][0].transpose(2, 0, 1).reshape(P, 8 * P),
    }
    arrays = {n: np.ascontiguousarray(v) for n, v in arrays.items()}
    nc = bacc.Bacc("TRN2", target_bir_lowering=False, num_devices=1)
    args = [nc.dram_tensor(f"in_{n}", arrays[n].shape, F32, kind="ExternalInput").ap() for n in _INS]
    out = nc.dram_tensor("out_t", (P, KT, T), F32, kind="ExternalOutput").ap()
    build(nc, *args, out)
    r = run(nc, [{f"in_{n}": v for n, v in arrays.items()}], core_ids=[0])
    return r.results[0]["out_t"].transpose(1, 0, 2).reshape(1, D, T).transpose(0, 2, 1)
```
